# Optimizing a Trainium2 kernel written in Bass

```python
import jax, jax.numpy as jnp
from jax import lax
import numpy as np

D_MODEL = 1024
BATCH = 1
SEQ = 1024
DEPTH = 1

SB_HEADS = 8
SB_HEAD_DIM = D_MODEL // SB_HEADS
SB_WIDTH = SB_HEADS * SB_HEAD_DIM
SB_BLOCK = 128
HG_HEADS = 8
HG_KEY_DIM = 128
HG_VAL_DIM = D_MODEL // HG_HEADS
HG_KEY_WIDTH = HG_HEADS * HG_KEY_DIM
HG_VAL_WIDTH = HG_HEADS * HG_VAL_DIM
HG_CHUNK = 64
N_BRANCHES = 2
RMS_EPS = 1e-6
IN_WIDTHS = (SB_WIDTH, SB_WIDTH, SB_WIDTH, SB_WIDTH,
             HG_KEY_WIDTH, HG_KEY_WIDTH, HG_VAL_WIDTH, HG_VAL_WIDTH,
             N_BRANCHES * D_MODEL)
IN_WIDTH = sum(IN_WIDTHS)

kernel_name = "hybrid_stickbreak_hgrn2_gated"

def rmsnorm(x, g):
    xf = x.astype(jnp.float32)
    y = xf * lax.rsqrt(jnp.mean(xf * xf, axis=-1, keepdims=True) + RMS_EPS)
    return (y * g.astype(jnp.float32)).astype(x.dtype)

def sb_attention(q, k, v):
    b, h, s, d = q.shape
    n_blocks = s // SB_BLOCK
    scale = d ** -0.5
    kf = k.astype(jnp.float32)
    vf = v.astype(jnp.float32)
    key_pos = jnp.arange(s)

    def block(i):
        start = i * SB_BLOCK
        qb = lax.dynamic_slice_in_dim(q, start, SB_BLOCK, axis=2).astype(jnp.float32)
        z = jnp.einsum('bhqd,bhkd->bhqk', qb, kf) * scale
        q_pos = start + jnp.arange(SB_BLOCK)
        causal = key_pos[None, :] < q_pos[:, None]
        log_not = jnp.where(causal, jax.nn.log_sigmoid(-z), 0.0)
        survive = lax.cumsum(log_not, axis=3, reverse=True) - log_not
        log_w = jnp.where(causal, jax.nn.log_sigmoid(z) + survive, -jnp.inf)
        w = jnp.exp(log_w)
        return jnp.einsum('bhqk,bhkd->bhqd', w, vf)

    out = lax.map(block, jnp.arange(n_blocks))
    out = jnp.transpose(out, (1, 2, 0, 3, 4)).reshape(b, h, s, d)
    return out.astype(q.dtype)

def hgrn2_chunked(q, k, g, v):
    b, s, h, dk = q.shape
    dv = v.shape[-1]
    n = s // HG_CHUNK

    def to_chunks(t):
        return t.reshape(b, n, HG_CHUNK, h, t.shape[-1]).transpose(1, 0, 3, 2, 4)

    causal = jnp.tril(jnp.ones((HG_CHUNK, HG_CHUNK), dtype=bool))[:, :, None]

    def step(state, inp):
        qc, kc, gc, vc = inp
        cum = jnp.cumsum(gc, axis=2)
        rel = cum[:, :, :, None, :] - cum[:, :, None, :, :]
        decay = jnp.exp(jnp.where(causal, rel, -jnp.inf))
        scores = jnp.einsum('bhtk,bhtsk,bhsk->bhts', qc, decay, kc)
        o = (jnp.einsum('bhts,bhsv->bhtv', scores, vc)
             + jnp.einsum('bhtk,bhkv->bhtv', qc * jnp.exp(cum), state))
        last = cum[:, :, -1:, :]
        state = (jnp.exp(last[:, :, 0, :])[..., None] * state
                 + jnp.einsum('bhsk,bhsv->bhkv', kc * jnp.exp(last - cum), vc))
        return state, o

    state0 = jnp.zeros((b, h, dk, dv), jnp.float32)
    _, o = lax.scan(step, state0, (to_chunks(q), to_chunks(k), to_chunks(g), to_chunks(v)))
    return o.transpose(1, 0, 3, 2, 4).reshape(b, s, h, dv)

def hybrid_layer(x, norm_g, w_in, b_gate, lb, hg_norm_g, w_sb_proj, w_hg_proj, w_out):
    b, s, _ = x.shape
    h = rmsnorm(x, norm_g)
    proj = jnp.einsum('bsd,de->bse', h, w_in)
    split_points = tuple(int(p) for p in np.cumsum(IN_WIDTHS)[:-1])
    sb_q, sb_k, sb_v, sb_z, hg_q, hg_f, hg_i, hg_z, gate_logits = jnp.split(proj, split_points, axis=-1)

    def heads(t):
        return t.reshape(b, s, SB_HEADS, SB_HEAD_DIM).transpose(0, 2, 1, 3)
    sb_o = sb_attention(heads(sb_q), heads(sb_k), heads(sb_v))
    sb_o = sb_o.transpose(0, 2, 1, 3).reshape(b, s, SB_WIDTH)
    u_sb = jnp.einsum('bse,ed->bsd', sb_o * jax.nn.silu(sb_z), w_sb_proj)

    f_logit = hg_f.reshape(b, s, HG_HEADS, HG_KEY_DIM).astype(jnp.float32)
    f = lb + (1.0 - lb) * jax.nn.sigmoid(f_logit)
    g = jnp.log(f)
    kk = 1.0 - f
    qq = jax.nn.silu(hg_q.reshape(b, s, HG_HEADS, HG_KEY_DIM).astype(jnp.float32))
    vv = hg_i.reshape(b, s, HG_HEADS, HG_VAL_DIM).astype(jnp.float32)
    hg_o = hgrn2_chunked(qq, kk, g, vv)
    hg_o = rmsnorm(hg_o, hg_norm_g).reshape(b, s, HG_VAL_WIDTH).astype(x.dtype)
    u_hg = jnp.einsum('bse,ed->bsd', hg_o * jax.nn.silu(hg_z), w_hg_proj)

    gates = jax.nn.sigmoid((gate_logits + b_gate).astype(jnp.float32)).astype(x.dtype)
    gate_sb, gate_hg = jnp.split(gates, N_BRANCHES, axis=-1)
    y = gate_sb * u_sb + gate_hg * u_hg
    return x + jnp.einsum('bsd,de->bse', y, w_out)

def setup_inputs(seed: int = 0) -> dict:
    key = jax.random.key(seed)
    ks = jax.random.split(key, 11)
    f32 = jnp.float32
    x = jax.random.normal(ks[0], (BATCH, SEQ, D_MODEL), f32)
    norm_g = 1.0 + 0.02 * jax.random.normal(ks[1], (DEPTH, D_MODEL), f32)
    w_in = jax.random.normal(ks[2], (DEPTH, D_MODEL, IN_WIDTH), f32) * D_MODEL ** -0.5
    b_gate = 0.1 * jax.random.normal(ks[3], (DEPTH, N_BRANCHES * D_MODEL), f32)
    lb_logits = 0.5 * jax.random.normal(ks[4], (DEPTH + 1, HG_HEADS, HG_KEY_DIM), f32)
    hg_norm_g = 1.0 + 0.02 * jax.random.normal(ks[5], (DEPTH, HG_HEADS, HG_VAL_DIM), f32)
    w_sb_proj = jax.random.normal(ks[6], (DEPTH, SB_WIDTH, D_MODEL), f32) * SB_WIDTH ** -0.5
    w_hg_proj = jax.random.normal(ks[7], (DEPTH, HG_VAL_WIDTH, D_MODEL), f32) * HG_VAL_WIDTH ** -0.5
    w_out = jax.random.normal(ks[8], (DEPTH, D_MODEL, D_MODEL), f32) * D_MODEL ** -0.5
    final_norm_g = 1.0 + 0.02 * jax.random.normal(ks[9], (D_MODEL,), f32)
    return {"x": x, "norm_g": norm_g, "w_in": w_in, "b_gate": b_gate, "lb_logits": lb_logits,
            "hg_norm_g": hg_norm_g, "w_sb_proj": w_sb_proj, "w_hg_proj": w_hg_proj,
            "w_out": w_out, "final_norm_g": final_norm_g}

def reference(x, norm_g, w_in, b_gate, lb_logits, hg_norm_g, w_sb_proj, w_hg_proj, w_out, final_norm_g):
    lb_all = jnp.cumsum(jax.nn.softmax(lb_logits.astype(jnp.float32), axis=0), axis=0)
    for l in range(DEPTH):
        x = hybrid_layer(x, norm_g[l], w_in[l], b_gate[l], lb_all[l], hg_norm_g[l],
                         w_sb_proj[l], w_hg_proj[l], w_out[l])
    return rmsnorm(x, final_norm_g)


_drawn_inputs = setup_inputs


def setup_inputs(seed=0):
    import zlib

    import numpy as np

    out = dict(_drawn_inputs(seed))
    spreads = {}
    factors = {'norm_g': 4.786,
     'b_gate': 4.224,
     'lb_logits': 3.246,
     'hg_norm_g': 8.0,
     'final_norm_g': 2.849}
    for name, (base, spread) in spreads.items():
        noise = np.random.default_rng([zlib.crc32(name.encode()), seed]).standard_normal(out[name].shape)
        drawn = base * np.exp(spread * noise) if base else spread * noise
        out[name] = __import__('jax').numpy.asarray(drawn.astype(out[name].dtype))
    for name, factor in factors.items():
        out[name] = (out[name] * factor).astype(out[name].dtype)
    return out
```

```python
from contextlib import ExitStack

import concourse.bass as bass
from concourse import mybir

F32 = mybir.dt.float32
F32R = mybir.dt.float32r
BF16 = mybir.dt.bfloat16
I32 = mybir.dt.int32
ACT = mybir.ActivationFunctionType
ALU = mybir.AluOpType

P = 128
D = 1024
S = 1024
KT = D // P
NT = S // P
HEADS = 8
HALF = S // 2
SLOTS = 16
EPS = 1e-6
SB_SCALE = float(P) ** -0.5
LEVELS = 7
CONSTANTS = 9 + 2 * LEVELS
SBUF_BASE = 16512

SB_Q, SB_K, SB_V, SB_Z, HG_Q, HG_F, HG_I, HG_Z, GATES = range(9)
HEAD_PANELS = (SB_Q, SB_K, HG_Q, HG_F, SB_Z, HG_Z, SB_V, HG_I)
PANEL_SLOT = (0, 1, 0, 1, 0, 1, 2, 3)
GATE_STEP = HEADS
N_GATE_PANELS = 2 * D // P
N_HEAD_PANELS = HEADS * len(HEAD_PANELS)
SB_PANEL0 = N_HEAD_PANELS + N_GATE_PANELS
HG_PANEL0 = SB_PANEL0 + D // P
OUT_PANEL0 = HG_PANEL0 + D // P
TAIL_SLOT0 = 10 * SLOTS

HEAD_SPLITS = {0: 1, 2: 2, 4: 3, 6: 4, 8: 5, 10: 6, 11: 7, 12: 8}
GATE_SPLITS = {0: 1, 2: 2, 4: 3, 6: 4, 8: 5, 10: 6, 12: 7, 14: 8}

OUT_COLUMNS = (0, 2, 3, 1, 4, 5, 6, 7)

QK_SLOT = {0: 0, 1: 1, 2: 2, 3: 3, 5: 4, 7: 5, 9: 6, 11: 7}
TR_SLOT = {1: 0, 2: 1, 3: 2, 4: 3, 7: 4, 9: 5, 11: 6, 13: 7}
PV_SLOT = {2: 0, 3: 1, 4: 2, 5: 3, 8: 4, 10: 5, 12: 6, 14: 7}


def tr_group(j, part):
    return j if j < 4 else 4 + 2 * (j - 4) + part


def need(engine, semaphore, value):
    if isinstance(value, int) and value <= 0:
        return
    engine.wait_ge(semaphore, value)


def build(nc, x, norm_g, w_in, b_gate, lb_logits, hg_norm_g, w_sb, w_hg, w_out, final_g, out):
    ctx = ExitStack()
    with ctx:
        def sem(name):
            return ctx.enter_context(nc.semaphore(name))

        def place(name, offset, free, dt=F32):
            return nc.alloc_sbuf_tensor_at(name, [P] + list(free), dt, offset=SBUF_BASE + offset)

        KB = 1024
        hT_hi = place("hT_hi", 0, [KT, S], F32R)
        hT_lo = place("hT_lo", 32 * KB, [KT, S], F32R)
        ohg_hi = place("ohg_hi", 0, [KT, S], F32R)
        ohg_lo = place("ohg_lo", 32 * KB, [KT, S], F32R)
        wo_hi = place("wo_hi", 0, [4, KT, P], F32R)
        wo_lo = place("wo_lo", 16 * KB, [4, KT, P], F32R)
        x_again = place("x_again", 32 * KB, [NT, D])
        w_raw = place("w_raw", 64 * KB, [2, KT, P])
        w_hi = place("w_hi", 72 * KB, [4, KT, P], F32R)
        w_lo = place("w_lo", 88 * KB, [4, KT, P], F32R)
        WORK = 104 * KB
        SET = 36 * KB

        def in_sets(name, at, free):
            return [place(f"{name}{i}", WORK + i * SET + at * KB, free) for i in range(2)]

        qT = in_sets("qT", 0, [S])
        kT = in_sets("kT", 4, [S])
        vv = in_sets("vv", 8, [NT, 2, P])
        zT = in_sets("zT", 16, [S])
        hzT = in_sets("hzT", 20, [S])
        hq = in_sets("hq", 24, [S])
        hk = in_sets("hk", 28, [S])
        forget = in_sets("forget", 32, [S])
        at = WORK + 2 * SET
        beta = place("beta", at, [S])
        kappa = place("kappa", at + 4096, [S + 1])
        wT = place("wT", at + 8224, [2, NT, P])
        scT = place("scT", at + 16416, [S])
        sb_parts = place("sb_parts", at + 20512, [2, HALF], F32R)
        hg_parts = place("hg_parts", at + 24608, [2, HALF], F32R)
        at += 28704
        ident = place("ident", at, [P])
        mean_w = place("mean_w", at + 512, [P])
        level_mask = place("level_mask", at + 1024, [LEVELS, P // 2])
        at += 1024 + LEVELS * 256
        ng = place("ng", at, [KT])
        lb = place("lb", at + 32, [HEADS])
        one_m_lb = place("one_m_lb", at + 64, [HEADS])
        hgn = place("hgn", at + 96, [HEADS])
        bg = place("bg", at + 128, [N_GATE_PANELS])
        chunk_total = place("chunk_total", at + 192, [NT])
        rstd = place("rstd", at + 224, [NT])
        lb_in = place("lb_in", at + 256, [2, HEADS])
        before = place("before", at + 320, [P], BF16)
        not_before = place("not_before", at + 576, [P], BF16)
        x_tok = place("x_tok", WORK, [NT, D])
        square_dump = place("square_dump", WORK + 32 * KB, [D])
        osb_hi = place("osb_hi", WORK, [KT, S], F32R)
        osb_lo = place("osb_lo", WORK + 32 * KB, [KT, S], F32R)
        y_hi = place("y_hi", WORK, [KT, S], F32R)
        y_lo = place("y_lo", WORK + 32 * KB, [KT, S], F32R)
        y_sum = place("y_sum", WORK + 64 * KB, [KT, S])
        res = place("res", WORK + 64 * KB, [NT, D])
        gate_in = place("gate_in", WORK + 96 * KB, [2, HALF])
        fg = place("fg", WORK + 96 * KB, [D])
        last_dump = place("last_dump", 64 * KB, [D])
        gate_out = [place("gate_out0", WORK, [2, HALF]), place("gate_out1", WORK + 64 * KB, [2, HALF])]

        osb_d = nc.dram_tensor("osb_d", (HEADS, P, 2, S), F32, kind="Internal").ap()
        ohg_d = nc.dram_tensor("ohg_d", (HEADS, P, 2, S), F32, kind="Internal").ap()
        gate_d = nc.dram_tensor("gate_d", (N_GATE_PANELS, P, S), F32, kind="Internal").ap()

        banks = ctx.enter_context(nc.psum_tensor("banks", [P, 8, HALF], F32))
        pj = [banks[:, 0, :], banks[:, 1, :]]
        score = banks[:, 2:4, :].rearrange("p a n -> p (a n)")
        turned = banks[:, 4, :]
        attended = banks[:, 5, :]
        hb = banks[:, 6:8, :].rearrange("p a n -> p (a n)")

        x_in = [sem(f"x_in{i}") for i in range(NT)]
        small_in = sem("small_in")
        const_made = sem("const_made")
        ss_done = sem("ss_done")
        rms_x = sem("rms_x")
        rstd_ready = sem("rstd_ready")
        xn_ready = sem("xn_ready")
        xT_done = sem("xT_done")
        hT_hi_ready = sem("hT_hi_ready")
        hT_ready = sem("hT_ready")
        lb_step = sem("lb_step")
        w_loaded = [sem("w_loaded0"), sem("w_loaded1")]
        w_hi_ready = sem("w_hi_ready")
        w_ready = sem("w_ready")
        proj_done = sem("proj_done")
        proj_sig = sem("proj_sig")
        proj_free = [sem("proj_free0"), sem("proj_free1")]
        forget_ready = sem("forget_ready")
        hk_ready = sem("hk_ready")
        qk_done = sem("qk_done")
        sig_done = sem("sig_done")
        masked = sem("masked")
        scan_done = sem("scan_done")
        w_done = sem("w_done")
        wtr_done = sem("wtr_done")
        wT_ready = sem("wT_ready")
        pv_done = sem("pv_done")
        sb_taken = sem("sb_taken")
        sb_hi = sem("sb_hi")
        sb_split = sem("sb_split")
        sb_stored = sem("sb_stored")
        hs_done = sem("hs_done")
        hs_taken = sem("hs_taken")
        grown = sem("grown")
        decayed = sem("decayed")
        ktr_done = sem("ktr_done")
        kt_ready = sem("kt_ready")
        kv_done = sem("kv_done")
        state_step = sem("state_step")
        ho_done = sem("ho_done")
        sq_done = sem("sq_done")
        on_done = sem("on_done")
        hn_done = sem("hn_done")
        rms_done = sem("rms_done")
        hg_norm = sem("hg_norm")
        hg_hi = sem("hg_hi")
        hg_split = sem("hg_split")
        hg_stored = sem("hg_stored")
        gate_made = sem("gate_made")
        gate_stored = [sem("gate_stored0"), sem("gate_stored1")]
        osb_in = sem("osb_in")
        ohg_in = sem("ohg_in")
        gate_loaded = [sem("gate_loaded0"), sem("gate_loaded1")]
        gated = sem("gated")
        y_part = sem("y_part")
        y_hi_ready = sem("y_hi_ready")
        y_ready = sem("y_ready")
        x_again_in = sem("x_again_in")
        fg_in = sem("fg_in")
        out_done = sem("out_done")
        res_ready = sem("res_ready")
        res_ss = sem("res_ss")
        res_rms = sem("res_rms")
        res_rstd = sem("res_rstd")
        normed = sem("normed")
        stored = sem("stored")

        block = ctx.enter_context(nc.Block())

        def halfs(t, b):
            return t[:, b * HALF:(b + 1) * HALF]

        def out_weights(column):
            if column < 4:
                return w_hi[:, column, :, :], w_lo[:, column, :, :]
            return wo_hi[:, column - 4, :, :], wo_lo[:, column - 4, :, :]

        def by_rows(w):
            return w.rearrange("(k p) e -> p k e", p=P)

        @block.sync
        def _(sp):
            for i in range(NT):
                sp.dma_start(x_tok[:, i, :], x[0, i * P:(i + 1) * P, :]).then_inc(x_in[i], 16)

            def load_panel(n_before, parity, source, first):
                need(sp, w_ready, n_before)
                sp.dma_start(w_raw[:, parity, :, :], by_rows(source)[:, :, bass.ds(first, P)]).then_inc(w_loaded[parity], 16)

            def load_head(h):
                for p, group in enumerate(HEAD_PANELS):
                    load_panel(8 * h + p - 1, p % 2, w_in[0], group * D + h * P)

            load_head(0)
            load_head(1)
            with sp.Fori(0, 3) as i:
                load_head(2 * i + 2)
                load_head(2 * i + 3)
            for p in range(N_GATE_PANELS):
                load_panel(N_HEAD_PANELS + p - 1, p % 2, w_in[0], GATES * D + p * P)
            for first, source in ((SB_PANEL0, w_sb[0]), (HG_PANEL0, w_hg[0])):
                with sp.Fori(0, D // P // 2) as i:
                    for c in range(2):
                        load_panel(2 * i + (first + c - 1), c, source, (2 * i + c) * P)
            for e, column in enumerate(OUT_COLUMNS):
                load_panel(OUT_PANEL0 + e - 1, e % 2, w_out[0], column * P)
                if e == 3:
                    sp.wait_ge(proj_done, TAIL_SLOT0 + 4 * KT)
                    for i in range(NT):
                        sp.dma_start(x_again[:, i, :], x[0, i * P:(i + 1) * P, :]).then_inc(x_again_in, 16)
                    sp.wait_ge(gated, 4 * KT)
                    sp.dma_start(fg[:, :], final_g.rearrange("(a n) -> a n", a=1).broadcast_to([P, D])).then_inc(fg_in, 16)
            for i in range(NT):
                sp.wait_ge(normed, i + 1)
                sp.dma_start(out[0, i * P:(i + 1) * P, :], res[:, i, :]).then_inc(stored, 16)
            sp.wait_ge(stored, 16 * NT)

        @block.gpsimd
        def _(pool):
            nc.gpsimd.memset(ident[:, :], 0.0).then_inc(const_made, 1)
            nc.gpsimd.memset(mean_w[:, :], 1.0 / P).then_inc(const_made, 1)
            nc.gpsimd.memset(kappa[:, S:S + 1], 1.0).then_inc(const_made, 1)
            nc.gpsimd.memset(level_mask[:, :, :], 1.0).then_inc(const_made, 1)
            nc.gpsimd.memset(before[:, :], 1.0).then_inc(const_made, 1)
            nc.gpsimd.memset(not_before[:, :], 0.0).then_inc(const_made, 1)
            pool.wait_ge(const_made, 6)
            nc.gpsimd.affine_select(out=ident[:, :], in_=ident[:, :], compare_op=ALU.not_equal, fill=1.0,
                                    base=0, pattern=[[-1, P]], channel_multiplier=1).then_inc(const_made, 1)
            nc.gpsimd.affine_select(out=before[:, :], in_=before[:, :], compare_op=ALU.is_gt, fill=0.0,
                                    base=0, pattern=[[-1, P]], channel_multiplier=1).then_inc(const_made, 1)
            nc.gpsimd.affine_select(out=not_before[:, :], in_=not_before[:, :], compare_op=ALU.is_gt, fill=1.0,
                                    base=0, pattern=[[-1, P]], channel_multiplier=1).then_inc(const_made, 1)
            made = 9
            for level in range(LEVELS):
                size = 1 << level
                pairs = P // 2 // size
                view = level_mask[:, level, :].rearrange("p (i b) -> p i b", b=size)
                nc.gpsimd.affine_select(out=view, in_=view, compare_op=ALU.is_ge, fill=0.0, base=0,
                                        pattern=[[-2 * size, pairs], [0, size]], channel_multiplier=1).then_inc(const_made, 1)
                made += 1
                pool.wait_ge(const_made, made)
                nc.gpsimd.affine_select(out=view, in_=view, compare_op=ALU.is_gt, fill=0.0, base=size,
                                        pattern=[[2 * size, pairs], [0, size]], channel_multiplier=-1).then_inc(const_made, 1)
                made += 1
            pool.wait_ge(const_made, made)

            def split(n, parity, slot):
                pool.wait_ge(w_hi_ready, n + 1)
                nc.gpsimd.tensor_tensor(w_lo[:, slot, :, :], w_raw[:, parity, :, :],
                                        w_hi[:, slot, :, :].bitcast(F32), ALU.subtract).then_inc(w_ready, 1)

            def split_out(e):
                pool.wait_ge(w_hi_ready, OUT_PANEL0 + e + 1)
                hi, lo = out_weights(OUT_COLUMNS[e])
                nc.gpsimd.tensor_tensor(lo, w_raw[:, e % 2, :, :], hi.bitcast(F32), ALU.subtract).then_inc(w_ready, 1)

            def step(h, splits):
                for u in range(SLOTS):
                    if u in splits:
                        p = splits[u]
                        slot = PANEL_SLOT[p] if splits is HEAD_SPLITS and p < 8 else p % 2
                        split(8 * h + p, p % 2, slot)

            split(0, 0, 0)
            step(0, HEAD_SPLITS)
            step(1, HEAD_SPLITS)
            with pool.Fori(0, 3) as i:
                step(2 * i + 2, HEAD_SPLITS)
                step(2 * i + 3, HEAD_SPLITS)
            step(GATE_STEP, GATE_SPLITS)
            step(GATE_STEP + 1, GATE_SPLITS)
            with pool.Fori(0, 2 * KT // 2) as i:
                split(2 * i + (SB_PANEL0 + 1), 1, 1)
                split(2 * i + (SB_PANEL0 + 2), 0, 0)
            for e in range(1, KT):
                split_out(e)


        @block.scalar
        def _(act):
            with nc.allow_non_contiguous_dma(reason="gains and biases, one value to a partition"):
                for dst, src in ((ng[:, :], norm_g[0].rearrange("(k p) -> p k", p=P)),
                                 (bg[:, :], b_gate[0].rearrange("(k p) -> p k", p=P)),
                                 (hgn[:, :], hg_norm_g[0].rearrange("h p -> p h")),
                                 (lb_in[:, 0, :], lb_logits[0].rearrange("h p -> p h")),
                                 (lb_in[:, 1, :], lb_logits[1].rearrange("h p -> p h"))):
                    act.dma_start(dst, src).then_inc(small_in, 16)

            def split(parity, slot, loads_before):
                act.wait_ge(w_loaded[parity], 16 * loads_before + 16)
                nc.scalar.activation(w_hi[:, slot, :, :], w_raw[:, parity, :, :], ACT.Copy).then_inc(w_hi_ready, 1)

            for i in range(NT):
                act.wait_ge(x_in[i], 16)
                need(act, ss_done, i)
                nc.scalar.activation(square_dump[:, :], x_tok[:, i, :], ACT.Square,
                                     accum_out=rstd[:, i:i + 1]).then_inc(ss_done, 1)
            act.wait_ge(ss_done, NT)
            nc.scalar.activation(rstd[:, :], rstd[:, :], ACT.Sqrt, scale=1.0 / D, bias=EPS).then_inc(rms_x, 1)
            for g in range(SLOTS):
                b, k = g // KT, g % KT
                act.wait_ge(xT_done, g + 1)
                if g == 0:
                    act.wait_ge(small_in, 16 * 5)
                nc.scalar.activation(halfs(hT_hi[:, k, :], b), banks[:, g % 8, :], ACT.Copy,
                                     scale=ng[:, k:k + 1]).then_inc(hT_hi_ready, 1)
            act.wait_ge(lb_step, 1)
            nc.scalar.activation(lb[:, :], lb_in[:, 0, :], ACT.Sigmoid).then_inc(lb_step, 1)
            split(0, 0, 0)

            def evacuate(h, u, s):
                p, b = u // 2, u % 2
                act.wait_ge(proj_done, 16 * h + u + 1)
                if u == 0:
                    need(act, sb_split, 2 * (h - 1))
                group = HEAD_PANELS[p]
                if group in (SB_Q, SB_K):
                    nc.scalar.activation(halfs((qT if group == SB_Q else kT)[s], b), pj[b], ACT.Copy).then_inc(proj_free[b], 1)
                elif group == HG_F:
                    nc.scalar.activation(halfs(forget[s], b), pj[b], ACT.Sigmoid).then_inc(proj_free[b], 1)
                elif group in (SB_V, HG_I):
                    t = 2 * (u - 12)
                    nc.scalar.activation(vv[s][:, t:t + 2, :, :], pj[b].rearrange("p (t g e) -> p t g e", t=2, g=2),
                                         ACT.Copy).then_inc(proj_free[b], 1)
                else:
                    dst = {HG_Q: hq, SB_Z: zT, HG_Z: hzT}[group][s]
                    nc.scalar.activation(halfs(dst, b), pj[b], ACT.Sigmoid).then_inc(proj_sig, 1)

            def make_gate(r, u):
                p, b = u // 2, u % 2
                act.wait_ge(proj_done, 16 * (GATE_STEP + r) + u + 1)
                if r == 0 and u == 0:
                    act.wait_ge(sb_split, 2 * (HEADS - 1))
                need(act, gate_stored[b], 16 * (8 * r + p))
                nc.scalar.activation(gate_out[r][:, b, :], pj[b], ACT.Sigmoid,
                                     bias=bg[:, 8 * r + p:8 * r + p + 1]).then_inc(proj_free[b], 1)
                act.wait_ge(proj_free[b], 8 * (GATE_STEP + r) + p + 1)
                act.dma_start(halfs(gate_d[8 * r + p], b), gate_out[r][:, b, :]).then_inc(gate_stored[b], 16)

            def take_turned(a, j, part):
                g = tr_group(j, part)
                first = 4 * part
                n = min(4, j + 1 - first)
                act.wait_ge(wtr_done, 12 * a + g + 1)
                need(act, pv_done, 8 * a + j - 1)
                nc.scalar.activation(wT[:, j % 2, first:first + n, :], turned[:, 0:n * P], ACT.Copy).then_inc(wT_ready, 1)

            def sigmoids(a, j):
                n = (j + 1) * P
                act.wait_ge(qk_done, 8 * a + j + 1)
                nc.scalar.activation(beta[:, S - n:S], score[:, 0:n], ACT.Sigmoid, scale=SB_SCALE)
                nc.scalar.activation(kappa[:, S - n:S], score[:, 0:n], ACT.Sigmoid, scale=-SB_SCALE).then_inc(sig_done, 1)

            def attend_hg(a, u, s):
                if u == 8:
                    act.wait_ge(ktr_done, a + 1)
                    for b in range(2):
                        nc.scalar.activation(halfs(forget[s], b), halfs(hb, b), ACT.Copy).then_inc(kt_ready, 1)
                if u == 11:
                    act.wait_ge(ho_done, a + 1)
                    for b in range(2):
                        nc.scalar.activation(halfs(scT, b), halfs(hb, b), ACT.Square).then_inc(sq_done, 1)
                if u == 12:
                    act.wait_ge(hn_done, a + 1)
                    for b in range(2):
                        nc.scalar.activation(halfs(scT, b), halfs(hb, b), ACT.Sqrt, bias=EPS).then_inc(rms_done, 1)

            def store(what, a, b):
                split_sem, stored_sem, parts, dram = {"sb": (sb_split, sb_stored, sb_parts, osb_d),
                                                      "hg": (hg_split, hg_stored, hg_parts, ohg_d)}[what]
                act.wait_ge(split_sem, 2 * a + b + 1)
                act.dma_start(dram[a][:, :, b * HALF:(b + 1) * HALF], parts[:, :, :].bitcast(F32)).then_inc(stored_sem, 16)

            def step(h, attend, s, stores_before=True):
                gates = isinstance(h, int) and h >= GATE_STEP
                splits = GATE_SPLITS if gates else HEAD_SPLITS
                for u in range(SLOTS):
                    if attend and u in TR_SLOT and TR_SLOT[u] >= 4:
                        take_turned(h - 1, TR_SLOT[u], 0)
                    if gates:
                        make_gate(h - GATE_STEP, u)
                    else:
                        evacuate(h, u, s)
                    if attend and u in TR_SLOT:
                        take_turned(h - 1, TR_SLOT[u], 1 if TR_SLOT[u] >= 4 else 0)
                    if u in splits:
                        p = splits[u]
                        split(p % 2, PANEL_SLOT[p] if p < 8 and not gates else p % 2, 4 * h + p // 2)
                    if attend and u in QK_SLOT:
                        sigmoids(h - 1, QK_SLOT[u])
                    if u == 0 and stores_before:
                        store("sb", h - 2, 1)
                    if attend:
                        attend_hg(h - 1, u, 1 - s)
                        if u == 7:
                            store("sb", h - 1, 0)
                        if u >= 14:
                            store("hg", h - 1, u - 14)

            step(0, False, 0, False)
            step(1, True, 1, False)
            with act.Fori(0, 3) as i:
                step(2 * i + 2, True, 0)
                step(2 * i + 3, True, 1)
            step(GATE_STEP, True, 0)
            store("sb", HEADS - 1, 1)
            act.wait_ge(sb_stored, 32 * HEADS)
            act.wait_ge(hg_split, 2 * HEADS)
            for e in range(HEADS):
                for part, dst in enumerate((osb_hi, osb_lo)):
                    act.dma_start(dst[:, e, :].bitcast(F32), osb_d[e][:, part, :]).then_inc(osb_in, 16)
            step(GATE_STEP + 1, False, 1, False)
            act.wait_ge(hg_stored, 32 * HEADS)
            for e in range(HEADS):
                for part, dst in enumerate((ohg_hi, ohg_lo)):
                    act.dma_start(dst[:, e, :].bitcast(F32), ohg_d[e][:, part, :]).then_inc(ohg_in, 16)
            for b in range(2):
                act.wait_ge(gate_stored[b], 16 * N_GATE_PANELS)
            for b in range(2):
                act.dma_start(gate_in[:, b, :], halfs(gate_d[0], b)).then_inc(gate_loaded[b], 16)

            def tail_panel(i, c, more):
                act.wait_ge(proj_done, 4 * i + (2 * c + TAIL_SLOT0))
                split(1 - c, 1 - c, i + (SB_PANEL0 // 2 + c))
                for b in range(2 if more else 0):
                    act.wait_ge(gated, 4 * i + (2 * c + b + 1))
                    act.dma_start(gate_in[:, b, :], gate_d[2 * i + (c + 1)][:, b * HALF:(b + 1) * HALF]).then_inc(gate_loaded[b], 16)

            with act.Fori(0, KT - 1) as i:
                tail_panel(i, 0, True)
                tail_panel(i, 1, True)
            tail_panel(KT - 1, 0, True)
            tail_panel(KT - 1, 1, False)
            for e in range(1, KT):
                if e == 3:
                    act.wait_ge(proj_done, TAIL_SLOT0 + 4 * KT)
                act.wait_ge(w_loaded[e % 2], 16 * ((OUT_PANEL0 + e) // 2) + 16)
                nc.scalar.activation(out_weights(OUT_COLUMNS[e])[0], w_raw[:, e % 2, :, :], ACT.Copy).then_inc(w_hi_ready, 1)
            for i in range(NT):
                act.wait_ge(res_ready, NT + i + 1)
                need(act, res_ss, i)
                nc.scalar.activation(last_dump[:, :], res[:, i, :], ACT.Square, accum_out=rstd[:, i:i + 1]).then_inc(res_ss, 1)
                act.wait_ge(res_ss, i + 1)
                nc.scalar.activation(rstd[:, i:i + 1], rstd[:, i:i + 1], ACT.Sqrt, scale=1.0 / D, bias=EPS).then_inc(res_rms, 1)

        @block.vector
        def _(dve):
            v = nc.vector
            dve.wait_ge(small_in, 16 * 5)
            v.tensor_tensor(lb_in[:, 0, :], lb_in[:, 0, :], lb_in[:, 1, :], ALU.subtract).then_inc(lb_step, 1)
            dve.wait_ge(rms_x, 1)
            v.reciprocal(rstd[:, :], rstd[:, :]).then_inc(rstd_ready, 1)
            dve.wait_ge(rstd_ready, 1)
            for i in range(NT):
                v.tensor_scalar(x_tok[:, i, :], x_tok[:, i, :], rstd[:, i:i + 1], None, ALU.mult).then_inc(xn_ready, 1)
            for g in range(SLOTS):
                b, k = g // KT, g % KT
                dve.wait_ge(hT_hi_ready, g + 1)
                v.scalar_tensor_tensor(out=halfs(hT_lo[:, k, :], b), in0=banks[:, g % 8, :], scalar=ng[:, k:k + 1],
                                       in1=halfs(hT_hi[:, k, :], b).bitcast(F32), op0=ALU.mult, op1=ALU.subtract).then_inc(hT_ready, 1)
            dve.wait_ge(lb_step, 2)
            v.tensor_scalar(one_m_lb[:, :], lb[:, :], -1.0, 1.0, ALU.mult, ALU.add).then_inc(lb_step, 1)
            dve.wait_ge(lb_step, 3)

            def evacuate(h, u, s):
                p, b = u // 2, u % 2
                group = HEAD_PANELS[p]
                if group in (HG_Q, SB_Z, HG_Z):
                    dve.wait_ge(proj_sig, 6 * h + {HG_Q: 0, SB_Z: 2, HG_Z: 4}[group] + b + 1)
                    dst = halfs({HG_Q: hq, SB_Z: zT, HG_Z: hzT}[group][s], b)
                    v.tensor_tensor(dst, pj[b], dst, ALU.mult).then_inc(proj_free[b], 1)
                elif group == HG_F:
                    dve.wait_ge(proj_free[b], 8 * h + p + 1)
                    f = halfs(forget[s], b)
                    v.tensor_scalar(f, f, one_m_lb[:, bass.ds(h, 1)], lb[:, bass.ds(h, 1)], ALU.mult, ALU.add).then_inc(forget_ready, 1)
                    dve.wait_ge(forget_ready, 2 * h + b + 1)
                    v.tensor_scalar(halfs(hk[s], b), f, -1.0, 1.0, ALU.mult, ALU.add).then_inc(hk_ready, 1)

            def weigh(a, j):
                n = (j + 1) * P
                dve.wait_ge(sig_done, 8 * a + j + 1)
                v.tensor_tensor(kappa[:, S - P:S], kappa[:, S - P:S], not_before[:, :], ALU.max).then_inc(masked, 1)
                v.tensor_tensor(beta[:, S - P:S], beta[:, S - P:S], before[:, :], ALU.mult).then_inc(masked, 1)
                dve.wait_ge(masked, 16 * a + 2 * j + 2)
                back = kappa[:, S - n:S][:, ::-1]
                v.tensor_tensor_scan(back, back, back, 1.0, ALU.mult, ALU.min).then_inc(scan_done, 1)
                dve.wait_ge(scan_done, 8 * a + j + 1)
                v.tensor_tensor(beta[:, S - n:S], beta[:, S - n:S], kappa[:, S - n + 1:S + 1], ALU.mult).then_inc(w_done, 1)

            def finish_sb(a, b, s):
                dve.wait_ge(pv_done, 8 * a + 4 * b + 4)
                o = halfs(qT[s], b)
                v.tensor_tensor(o, attended, halfs(zT[s], b), ALU.mult).then_inc(sb_taken, 1)
                dve.wait_ge(sb_taken, 2 * a + b + 1)
                need(dve, sb_stored, 32 * a + 16 * b)
                v.tensor_copy(sb_parts[:, 0, :], o).then_inc(sb_hi, 1)
                dve.wait_ge(sb_hi, 2 * a + b + 1)
                v.tensor_tensor(sb_parts[:, 1, :], o, sb_parts[:, 0, :].bitcast(F32), ALU.subtract).then_inc(sb_split, 1)

            def finish_hg(a, b, s):
                o = halfs(hq[s], b)
                need(dve, hg_stored, 32 * a + 16 * b)
                v.tensor_copy(hg_parts[:, 0, :], o).then_inc(hg_hi, 1)
                dve.wait_ge(hg_hi, 2 * a + b + 1)
                v.tensor_tensor(hg_parts[:, 1, :], o, hg_parts[:, 0, :].bitcast(F32), ALU.subtract).then_inc(hg_split, 1)

            def grow(a, m, s):
                size = 1 << (m - 1)
                pairs = S // (2 * size)

                def pairs_of(t):
                    return t[s][:, :].rearrange("p (c two b) -> p c two b", two=2, b=size)

                even, odd = (pairs_of(forget)[:, :, z, 0:1] for z in range(2))
                q_odd, k_even = pairs_of(hq)[:, :, 1, :], pairs_of(hk)[:, :, 0, :]
                v.tensor_tensor(q_odd, q_odd, even.broadcast_to([P, pairs, size]), ALU.mult).then_inc(grown, 1)
                v.tensor_tensor(k_even, k_even, odd.broadcast_to([P, pairs, size]), ALU.mult).then_inc(grown, 1)
                return even, odd

            def multiply_totals(a, m, even, odd):
                dve.wait_ge(grown, 14 * a + 2 * m)
                total = chunk_total[:, :].unsqueeze(2) if m == LEVELS else even
                v.tensor_tensor(total, even, odd, ALU.mult).then_inc(decayed, 1)

            def attend_hg(a, u, s):
                if u == 0:
                    dve.wait_ge(hs_done, 8 * a + 1)
                    v.tensor_tensor(scT[:, :].rearrange("p (n t) -> p n t", n=NT), hb.rearrange("p (n t) -> p n t", n=NT),
                                    ident[:, :].unsqueeze(1).broadcast_to([P, NT, P]), ALU.mult).then_inc(hs_taken, 1)
                    v.tensor_tensor(hq[s][:, :], hq[s][:, :], forget[s][:, :], ALU.mult).then_inc(decayed, 1)
                if 1 <= u <= LEVELS:
                    size = 1 << (u - 1)
                    dve.wait_ge(hs_done, 8 * a + u + 1)
                    dve.wait_ge(decayed, 8 * a + u)
                    even, odd = grow(a, u, s)
                    dve.wait_ge(const_made, CONSTANTS)
                    dve.wait_ge(hs_taken, 8 * a + u)
                    half = halfs(hb, (u + 1) % 2)
                    v.copy_predicated(scT[:, :].rearrange("p (n i two b) -> p n i two b", n=NT, two=2, b=size)[:, :, :, 1, :],
                                      level_mask[:, u - 1, :].bitcast(I32).rearrange("p (i b) -> p i b", b=size)
                                      .unsqueeze(1).broadcast_to([P, NT, P // 2 // size, size]),
                                      half.rearrange("p (n i b) -> p n i b", n=NT, b=size)).then_inc(hs_taken, 1)
                    multiply_totals(a, u, even, odd)
                if u == 9:
                    dve.wait_ge(kv_done, a + 1)
                    dve.wait_ge(decayed, 8 * a + 8)
                    for n in range(NT - 1):
                        new, kv = hk[s][:, n * P:(n + 1) * P], hb[:, n * P:(n + 1) * P]
                        if n == 0:
                            v.tensor_copy(new, kv).then_inc(state_step, 1)
                        else:
                            dve.wait_ge(state_step, 7 * a + n)
                            v.scalar_tensor_tensor(out=new, in0=hk[s][:, (n - 1) * P:n * P], scalar=chunk_total[:, n:n + 1],
                                                   in1=kv, op0=ALU.mult, op1=ALU.add).then_inc(state_step, 1)
                if u == 11:
                    for b in range(2):
                        dve.wait_ge(sq_done, 2 * a + b + 1)
                        v.tensor_scalar(halfs(hq[s], b), halfs(hb, b), hgn[:, bass.ds(a, 1)], None, ALU.mult).then_inc(on_done, 1)
                if u == 12:
                    dve.wait_ge(rms_done, 2 * a + 2)
                    v.reciprocal(scT[:, :], scT[:, :]).then_inc(hg_norm, 1)
                    dve.wait_ge(hg_norm, 3 * a + 1)
                    dve.wait_ge(on_done, 2 * a + 2)
                    v.tensor_tensor(hq[s][:, :], hq[s][:, :], scT[:, :], ALU.mult).then_inc(hg_norm, 1)
                    dve.wait_ge(hg_norm, 3 * a + 2)
                    v.tensor_tensor(hq[s][:, :], hq[s][:, :], hzT[s][:, :], ALU.mult).then_inc(hg_norm, 1)
                    dve.wait_ge(hg_norm, 3 * a + 3)
                if u in (13, 14):
                    finish_hg(a, u - 13, s)

            def step(h, attend, s):
                for u in range(SLOTS):
                    if not (isinstance(h, int) and h >= GATE_STEP):
                        evacuate(h, u, s)
                    if attend:
                        if u in QK_SLOT:
                            weigh(h - 1, QK_SLOT[u])
                        attend_hg(h - 1, u, 1 - s)
                        if u == 6:
                            finish_sb(h - 1, 0, 1 - s)
                        if u == 15:
                            finish_sb(h - 1, 1, 1 - s)

            step(0, False, 0)
            step(1, True, 1)
            with dve.Fori(0, 3) as i:
                step(2 * i + 2, True, 0)
                step(2 * i + 3, True, 1)
            step(GATE_STEP, True, 0)

            for b in range(2):
                dve.wait_ge(gate_stored[b], 16 * N_GATE_PANELS)

            def gate_sb(t, b, load):
                dve.wait_ge(proj_done, 2 * t + (TAIL_SLOT0 + b + 1))
                dve.wait_ge(gate_loaded[b], 16 * t + 16)
                dst = y_sum[:, t, b * HALF:(b + 1) * HALF] if isinstance(t, int) else y_sum[:, bass.ds(t, 1), b * HALF:(b + 1) * HALF].rearrange("p a n -> p (a n)")
                v.tensor_tensor(dst, pj[b], gate_in[:, b, :], ALU.mult).then_inc(gated, 1)

            with dve.Fori(0, KT) as t:
                gate_sb(t, 0, None)
                gate_sb(t, 1, None)
            with dve.Fori(0, KT) as t:
                for b in range(2):
                    dve.wait_ge(proj_done, 2 * t + (TAIL_SLOT0 + 2 * KT + b + 1))
                    dve.wait_ge(gate_loaded[b], 16 * t + (16 * KT + 16))
                    v.tensor_tensor(gate_in[:, b, :], pj[b], gate_in[:, b, :], ALU.mult).then_inc(y_part, 1)
                    dve.wait_ge(y_part, 2 * t + (b + 1))

                    def part(y):
                        return y[:, bass.ds(t, 1), b * HALF:(b + 1) * HALF].rearrange("p a n -> p (a n)")

                    v.tensor_tensor(part(y_sum), part(y_sum), gate_in[:, b, :], ALU.add).then_inc(gated, 1)
                    dve.wait_ge(gated, 2 * t + (2 * KT + b + 1))
                    v.tensor_copy(part(y_hi), part(y_sum)).then_inc(y_hi_ready, 1)
                    dve.wait_ge(y_hi_ready, 2 * t + (b + 1))
                    v.tensor_tensor(part(y_lo), part(y_sum), part(y_hi).bitcast(F32), ALU.subtract).then_inc(y_ready, 1)

            dve.wait_ge(x_again_in, 16 * NT)
            dve.wait_ge(y_ready, 2 * KT)

            def last_norm(i):
                dve.wait_ge(res_rms, i + 1)
                v.reciprocal(rstd[:, i:i + 1], rstd[:, i:i + 1]).then_inc(res_rstd, 1)
                dve.wait_ge(res_rstd, i + 1)
                v.scalar_tensor_tensor(out=res[:, i, :], in0=res[:, i, :], scalar=rstd[:, i:i + 1], in1=fg[:, :],
                                       op0=ALU.mult, op1=ALU.mult).then_inc(normed, 1)

            dve.wait_ge(fg_in, 16)
            for g in range(2 * NT):
                c, i = g // NT, g % NT
                dve.wait_ge(out_done, g + 1)
                cols = slice(c * HALF, (c + 1) * HALF)
                v.tensor_tensor(res[:, i, cols], banks[:, g % 8, :], x_again[:, i, cols], ALU.add).then_inc(res_ready, 1)
                if g > NT:
                    last_norm(i - 1)
            last_norm(NT - 1)

        @block.tensor
        def _(pe):
            mm = nc.tensor.matmul
            pe.wait_ge(const_made, CONSTANTS)
            for g in range(SLOTS):
                b, k = g // KT, g % KT
                pe.wait_ge(xn_ready, 4 * b + 4)
                need(pe, hT_ready, g - 7)
                for i in range(4):
                    last = nc.tensor.transpose(banks[:, g % 8, i * P:(i + 1) * P], x_tok[:, 4 * b + i, k * P:(k + 1) * P], ident[:, :])
                last.then_inc(xT_done, 1)
            pe.wait_ge(hT_ready, SLOTS)

            def feature_major(b, slot, hi, lo):
                for k in range(KT):
                    for z, (w, t) in enumerate(((w_hi, hi), (w_hi, lo), (w_lo, hi))):
                        last = mm(pj[b], w[:, slot, k, :], halfs(t[:, k, :], b), start=k == 0 and z == 0, stop=k == KT - 1 and z == 2)
                return last

            def token_major(b, t):
                for i in range(2):
                    dst = pj[b][:, i * 2 * P:(i + 1) * 2 * P].rearrange("p (g e) -> p g e", g=2)
                    for k in range(KT):
                        for z, (hh, w) in enumerate(((hT_hi, w_hi), (hT_lo, w_hi), (hT_hi, w_lo))):
                            last = mm(dst, hh[:, k, (t + i) * P:(t + i + 1) * P], w[:, 2:4, k, :],
                                      start=k == 0 and z == 0, stop=k == KT - 1 and z == 2)
                return last

            def project(h, u, gates):
                p, b = u // 2, u % 2
                need(pe, proj_free[b], 8 * h + p)
                if u % 2 == 0:
                    pe.wait_ge(w_ready, 8 * h + p + (2 if u == 12 and not gates else 1))
                if u >= 12 and not gates:
                    last = token_major(b, 2 * (u - 12))
                else:
                    last = feature_major(b, p % 2, hT_hi, hT_lo)
                last.then_inc(proj_done, 1)

            def scores(a, j, s):
                if j > 0:
                    pe.wait_ge(sig_done, 8 * a + j)
                n = (j + 1) * P
                for at in range(0, n, HALF):
                    m = min(HALF, n - at)
                    last = mm(score[:, at:at + m], qT[s][:, j * P:(j + 1) * P], kT[s][:, at:at + m], start=True, stop=True)
                last.then_inc(qk_done, 1)

            def turn(a, j, part):
                g = tr_group(j, part)
                pe.wait_ge(w_done, 8 * a + j + 1)
                need(pe, wT_ready, 12 * a + g)
                n = (j + 1) * P
                for i in range(4 * part, min(4 * part + 4, j + 1)):
                    last = nc.tensor.transpose(turned[:, (i % 4) * P:(i % 4 + 1) * P], beta[:, S - n + i * P:S - n + (i + 1) * P], ident[:, :])
                last.then_inc(wtr_done, 1)

            def attend_sb(a, j, s):
                pe.wait_ge(wT_ready, 12 * a + tr_group(j, 1 if j >= 4 else 0) + 1)
                if j % 4 == 0:
                    need(pe, sb_taken, 2 * a + j // 4)
                for i in range(j + 1):
                    last = mm(attended[:, (j % 4) * P:(j % 4 + 1) * P], vv[s][:, i, 0, :], wT[:, j % 2, i, :], start=i == 0, stop=i == j)
                last.then_inc(pv_done, 1)

            def attend_hg(a, u, s):
                def tile(t, n):
                    return t[:, n * P:(n + 1) * P]

                if u == 0:
                    pe.wait_ge(hk_ready, 2 * a + 2)
                    need(pe, rms_done, 2 * a)
                    for n in range(NT):
                        last = mm(tile(hb, n), tile(hk[s], n), tile(hq[s], n), start=True, stop=True)
                    last.then_inc(hs_done, 1)
                if 1 <= u <= LEVELS:
                    size = 1 << (u - 1)
                    pe.wait_ge(decayed, 8 * a + u)
                    pe.wait_ge(hs_taken, 8 * a + max(1, u - 1))
                    half = halfs(hb, (u + 1) % 2)
                    for n in range(NT):
                        odd = tile(hq[s], n).rearrange("p (i two b) -> p i two b", two=2, b=size)[:, :, 1, :]
                        last = mm(half[:, n * 64:(n + 1) * 64].rearrange("p (i b) -> p i b", b=size), tile(hk[s], n), odd,
                                  start=True, stop=True)
                    last.then_inc(hs_done, 1)
                if u == 8:
                    pe.wait_ge(decayed, 8 * a + 8)
                    pe.wait_ge(hs_taken, 8 * a + 8)
                    for n in range(NT):
                        last = nc.tensor.transpose(tile(hb, n), tile(hk[s], n), ident[:, :])
                    last.then_inc(ktr_done, 1)
                if u == 9:
                    pe.wait_ge(kt_ready, 2 * a + 2)
                    for n in range(NT - 1):
                        last = mm(tile(hb, n), tile(forget[s], n), vv[s][:, n, 1, :], start=True, stop=True)
                    last.then_inc(kv_done, 1)
                if u == 11:
                    pe.wait_ge(state_step, 7 * a + 7)
                    for n in range(NT):
                        last = mm(tile(hb, n), vv[s][:, n, 1, :], tile(scT, n), start=True, stop=n == 0)
                        if n:
                            last = mm(tile(hb, n), tile(hk[s], n - 1), tile(hq[s], n), start=False, stop=True)
                    last.then_inc(ho_done, 1)
                if u == 12:
                    pe.wait_ge(sq_done, 2 * a + 2)
                    pe.wait_ge(on_done, 2 * a + 2)
                    for b in range(2):
                        last = mm(halfs(hb, b), mean_w[:, :], halfs(scT, b), start=True, stop=True)
                    last.then_inc(hn_done, 1)

            def step(h, attend, s):
                gates = isinstance(h, int) and h >= GATE_STEP
                a, o = h - 1, 1 - s
                for u in range(SLOTS):
                    if attend and u in TR_SLOT and TR_SLOT[u] >= 4:
                        turn(a, TR_SLOT[u], 0)
                    project(h, u, gates)
                    if attend:
                        if u in TR_SLOT:
                            turn(a, TR_SLOT[u], 1 if TR_SLOT[u] >= 4 else 0)
                        if u in QK_SLOT:
                            scores(a, QK_SLOT[u], o)
                        if u in PV_SLOT:
                            attend_sb(a, PV_SLOT[u], o)
                        attend_hg(a, u, o)

            step(0, False, 0)
            step(1, True, 1)
            with pe.Fori(0, 3) as i:
                step(2 * i + 2, True, 0)
                step(2 * i + 3, True, 1)
            step(GATE_STEP, True, 0)
            step(GATE_STEP + 1, False, 1)

            def branch_panel(t, c, first, hi, lo):
                pe.wait_ge(w_ready, t + (SB_PANEL0 + first + 1))
                for b in range(2):
                    if not (isinstance(t, int) and t + first == 0):
                        pe.wait_ge(gated, 2 * t + (2 * first + b - 1))
                    else:
                        pe.wait_ge(proj_free[b], TAIL_SLOT0 // 2)
                    feature_major(b, c, hi, lo).then_inc(proj_done, 1)

            pe.wait_ge(osb_in, 16 * 2 * HEADS)
            branch_panel(0, 0, 0, osb_hi, osb_lo)
            branch_panel(1, 1, 0, osb_hi, osb_lo)
            with pe.Fori(0, KT // 2 - 1) as i:
                branch_panel(2 * i + 2, 0, 0, osb_hi, osb_lo)
                branch_panel(2 * i + 3, 1, 0, osb_hi, osb_lo)
            pe.wait_ge(ohg_in, 16 * 2 * HEADS)
            with pe.Fori(0, KT // 2) as i:
                branch_panel(2 * i, 0, KT, ohg_hi, ohg_lo)
                branch_panel(2 * i + 1, 1, KT, ohg_hi, ohg_lo)

            pe.wait_ge(y_ready, 2 * KT)
            for g in range(2 * NT):
                c, i = g // NT, g % NT
                if i == 0:
                    pe.wait_ge(w_ready, OUT_PANEL0 + 4 * (c + 1))
                need(pe, res_ready, g - 7)
                dst = banks[:, g % 8, :].rearrange("p (g e) -> p g e", g=4)
                for k in range(KT):
                    hi, lo = (w_hi, w_lo) if c == 0 else (wo_hi, wo_lo)
                    for z, (y, w) in enumerate(((y_hi, hi), (y_lo, hi), (y_hi, lo))):
                        last = mm(dst, y[:, k, i * P:(i + 1) * P], w[:, :, k, :], start=k == 0 and z == 0, stop=k == KT - 1 and z == 2)
                last.then_inc(out_done, 1)


_INS = ("x", "norm_g", "w_in", "b_gate", "lb_logits", "hg_norm_g", "w_sb_proj", "w_hg_proj", "w_out", "final_norm_g")


def kernel(**inputs):
    import numpy as np
    import concourse.bacc as bacc
    from concourse.bass_utils import run_bass_kernel_spmd

    nc = bacc.Bacc("TRN2", target_bir_lowering=False, num_devices=1)
    arrays = {f"in_{name}": np.ascontiguousarray(inputs[name]) for name in _INS}
    args = [nc.dram_tensor(name, a.shape, mybir.dt.from_np(a.dtype), kind="ExternalInput").ap() for name, a in arrays.items()]
    out = nc.dram_tensor("out", (1, S, D), F32, kind="ExternalOutput").ap()
    build(nc, *args, out)
    r = run_bass_kernel_spmd(nc, [arrays], core_ids=[0])
    return r.results[0]["out"]
```

```python
from contextlib import ExitStack

import concourse.bass as bass
from concourse import mybir

F32 = mybir.dt.float32
F32R = mybir.dt.float32r
BF16 = mybir.dt.bfloat16
I32 = mybir.dt.int32
ACT = mybir.ActivationFunctionType
ALU = mybir.AluOpType

P = 128
D = 1024
S = 1024
KT = D // P
NT = S // P
HEADS = 8
HALF = S // 2
SLOTS = 16
EPS = 1e-6
SB_SCALE = float(P) ** -0.5
LEVELS = 7
MASKED = 5
IDENT_MADE = 2
CONSTANTS = 9 + 2 * MASKED
SBUF_BASE = 16512

SB_Q, SB_K, SB_V, SB_Z, HG_Q, HG_F, HG_I, HG_Z, GATES = range(9)
HEAD_PANELS = (SB_Q, SB_K, HG_Q, HG_F, SB_Z, HG_Z, SB_V, HG_I)
PANEL_SLOT = (0, 1, 0, 1, 0, 1, 2, 3)
GATE_STEP = HEADS
N_GATE_PANELS = 2 * D // P
N_HEAD_PANELS = HEADS * len(HEAD_PANELS)
SB_PANEL0 = N_HEAD_PANELS + N_GATE_PANELS
HG_PANEL0 = SB_PANEL0 + D // P
OUT_PANEL0 = HG_PANEL0 + D // P
TAIL_SLOT0 = 10 * SLOTS

HEAD_SPLITS = {0: 1, 2: 2, 4: 3, 6: 4, 8: 5, 9: 6, 10: 7, 12: 8}
GATE_SPLITS = {0: 1, 2: 2, 4: 3, 6: 4, 8: 5, 10: 6, 12: 7, 14: 8}

START_ORDER = (0, 2, 1, 3) + tuple(range(4, SLOTS))

OUT_COLUMNS = (0, 2, 3, 1, 4, 5, 6, 7)

QK_SLOT = {0: 0, 1: 1, 2: 2, 3: 3, 5: 4, 7: 5, 9: 6, 11: 7}
TR_SLOT = {1: 0, 2: 1, 3: 2, 4: 3, 7: 4, 9: 5, 11: 6, 13: 7}
PV_SLOT = {2: 0, 3: 1, 4: 2, 5: 3, 8: 4, 10: 5, 12: 6, 14: 7}


def tr_group(j, part):
    return j if j < 4 else 4 + 2 * (j - 4) + part


def need(engine, semaphore, value):
    if isinstance(value, int) and value <= 0:
        return
    engine.wait_ge(semaphore, value)


def build(nc, x, norm_g, w_in, b_gate, lb_logits, hg_norm_g, w_sb, w_hg, w_out, final_g, out):
    ctx = ExitStack()
    with ctx:
        def sem(name):
            return ctx.enter_context(nc.semaphore(name))

        def place(name, offset, free, dt=F32):
            return nc.alloc_sbuf_tensor_at(name, [P] + list(free), dt, offset=SBUF_BASE + offset)

        KB = 1024
        hT_hi = place("hT_hi", 0, [KT, S], F32R)
        hT_lo = place("hT_lo", 32 * KB, [KT, S], F32R)
        ohg_hi = place("ohg_hi", 0, [KT, S], F32R)
        ohg_lo = place("ohg_lo", 32 * KB, [KT, S], F32R)
        wo_hi = place("wo_hi", 0, [4, KT, P], F32R)
        wo_lo = place("wo_lo", 16 * KB, [4, KT, P], F32R)
        x_again = place("x_again", 32 * KB, [NT, D])
        w_raw = place("w_raw", 64 * KB, [2, KT, P])
        w_hi = place("w_hi", 72 * KB, [4, KT, P], F32R)
        w_lo = place("w_lo", 88 * KB, [4, KT, P], F32R)
        WORK = 104 * KB
        SET = 36 * KB

        def in_sets(name, at, free):
            return [place(f"{name}{i}", WORK + i * SET + at * KB, free) for i in range(2)]

        qT = in_sets("qT", 0, [S])
        kT = in_sets("kT", 4, [S])
        vv = in_sets("vv", 8, [NT, 2, P])
        zT = in_sets("zT", 16, [S])
        hzT = in_sets("hzT", 20, [S])
        hq = in_sets("hq", 24, [S])
        hk = in_sets("hk", 28, [S])
        forget = in_sets("forget", 32, [S])
        sq_lo = [place(f"sq_lo{i}", WORK + i * SET + 28 * KB, [S], F32R) for i in range(2)]
        sq_hi = [place(f"sq_hi{i}", WORK + i * SET + 32 * KB, [S], F32R) for i in range(2)]
        at = WORK + 2 * SET
        beta = place("beta", at, [S])
        kappa = place("kappa", at + 4096, [S + 1])
        wT = place("wT", at + 8224, [2, NT, P])
        scT = place("scT", at + 16416, [S])
        sb_parts = place("sb_parts", at + 20512, [2, HALF], F32R)
        hg_parts = place("hg_parts", at + 24608, [2, HALF], F32R)
        at += 28704
        ident = place("ident", at, [P])
        mean_w = place("mean_w", at + 512, [P], F32R)
        level_mask = place("level_mask", at + 1024, [MASKED, P // 2])
        at += 1024 + MASKED * 256
        ng = place("ng", at, [KT])
        lb = place("lb", at + 32, [HEADS])
        one_m_lb = place("one_m_lb", at + 64, [HEADS])
        hgn = place("hgn", at + 96, [HEADS])
        bg = place("bg", at + 128, [N_GATE_PANELS])
        chunk_total = place("chunk_total", at + 192, [NT])
        rstd = place("rstd", at + 224, [NT])
        lb_in = place("lb_in", at + 256, [2, HEADS])
        before = place("before", at + 320, [P], BF16)
        not_before = place("not_before", at + 576, [P], BF16)
        x_tok = place("x_tok", WORK, [NT, D])
        square_dump = place("square_dump", WORK + 32 * KB, [D])
        osb_hi = place("osb_hi", WORK, [KT, S], F32R)
        osb_lo = place("osb_lo", WORK + 32 * KB, [KT, S], F32R)
        y_hi = place("y_hi", WORK, [KT, S], F32R)
        y_lo = place("y_lo", WORK + 32 * KB, [KT, S], F32R)
        y_sum = place("y_sum", WORK + 64 * KB, [KT, S])
        res = place("res", WORK + 64 * KB, [NT, D])
        gate_in = place("gate_in", WORK + 96 * KB, [2, HALF])
        fg = place("fg", WORK + 96 * KB, [D])
        last_dump = place("last_dump", 64 * KB, [D])
        gate_out = [place("gate_out0", WORK, [2, HALF]), place("gate_out1", WORK + 64 * KB, [2, HALF])]

        osb_d = nc.dram_tensor("osb_d", (HEADS, P, 2, S), F32, kind="Internal").ap()
        ohg_d = nc.dram_tensor("ohg_d", (HEADS, P, 2, S), F32, kind="Internal").ap()
        gate_d = nc.dram_tensor("gate_d", (N_GATE_PANELS, P, S), F32, kind="Internal").ap()

        banks = ctx.enter_context(nc.psum_tensor("banks", [P, 8, HALF], F32))
        pj = [banks[:, 0, :], banks[:, 1, :]]
        score = banks[:, 2:4, :].rearrange("p a n -> p (a n)")
        turned = banks[:, 4, :]
        attended = banks[:, 5, :]
        hb = banks[:, 6:8, :].rearrange("p a n -> p (a n)")

        x_in = [sem(f"x_in{i}") for i in range(NT)]
        small_in = sem("small_in")
        ng_in = sem("ng_in")
        const_made = sem("const_made")
        ss_done = sem("ss_done")
        rms_x = sem("rms_x")
        rstd_ready = sem("rstd_ready")
        xn_ready = sem("xn_ready")
        xT_done = sem("xT_done")
        hT_hi_ready = sem("hT_hi_ready")
        hT_ready = sem("hT_ready")
        lb_step = sem("lb_step")
        w_loaded = [sem("w_loaded0"), sem("w_loaded1")]
        w_hi_ready = sem("w_hi_ready")
        w_ready = sem("w_ready")
        proj_done = sem("proj_done")
        proj_sig = sem("proj_sig")
        proj_free = [sem("proj_free0"), sem("proj_free1")]
        forget_ready = sem("forget_ready")
        hk_ready = sem("hk_ready")
        qk_done = sem("qk_done")
        sig_done = sem("sig_done")
        masked = sem("masked")
        scan_done = sem("scan_done")
        w_done = sem("w_done")
        wtr_done = sem("wtr_done")
        wT_ready = sem("wT_ready")
        pv_done = sem("pv_done")
        sb_taken = sem("sb_taken")
        sb_hi = sem("sb_hi")
        sb_split = sem("sb_split")
        sb_stored = sem("sb_stored")
        hs_done = sem("hs_done")
        hs_taken = sem("hs_taken")
        grown = sem("grown")
        decayed = sem("decayed")
        ktr_done = sem("ktr_done")
        kt_ready = sem("kt_ready")
        kv_done = sem("kv_done")
        state_step = sem("state_step")
        ho_done = sem("ho_done")
        sq_done = sem("sq_done")
        sq_hi_ready = sem("sq_hi_ready")
        sq_split = sem("sq_split")
        on_done = sem("on_done")
        hn_done = sem("hn_done")
        rms_done = sem("rms_done")
        hg_norm = sem("hg_norm")
        hg_hi = sem("hg_hi")
        hg_split = sem("hg_split")
        hg_stored = sem("hg_stored")
        gate_made = sem("gate_made")
        gate_stored = [sem("gate_stored0"), sem("gate_stored1")]
        osb_in = sem("osb_in")
        ohg_in = sem("ohg_in")
        gate_loaded = [sem("gate_loaded0"), sem("gate_loaded1")]
        gated = sem("gated")
        y_part = sem("y_part")
        y_hi_ready = sem("y_hi_ready")
        y_ready = sem("y_ready")
        x_again_in = sem("x_again_in")
        fg_in = sem("fg_in")
        out_done = sem("out_done")
        res_ready = sem("res_ready")
        res_ss = sem("res_ss")
        res_rms = sem("res_rms")
        res_rstd = sem("res_rstd")
        normed = sem("normed")
        stored = sem("stored")

        block = ctx.enter_context(nc.Block())

        def halfs(t, b):
            return t[:, b * HALF:(b + 1) * HALF]

        def out_weights(column):
            if column < 4:
                return w_hi[:, column, :, :], w_lo[:, column, :, :]
            return wo_hi[:, column - 4, :, :], wo_lo[:, column - 4, :, :]

        def xT_bank(g):
            return banks[:, g if g < KT else 2 + (g - KT) % 6, :]

        def out_bank(g):
            return banks[:, (g + 2) % 8, :]

        def by_rows(w):
            return w.rearrange("(k p) e -> p k e", p=P)

        @block.sync
        def _(sp):
            def load_x(i):
                sp.dma_start(x_tok[:, i, :], x[0, i * P:(i + 1) * P, :]).then_inc(x_in[i], 16)

            def load_panel(n_before, parity, source, first):
                need(sp, w_ready, n_before)
                sp.dma_start(w_raw[:, parity, :, :], by_rows(source)[:, :, bass.ds(first, P)]).then_inc(w_loaded[parity], 16)

            def load_head(h, first=0):
                for p, group in enumerate(HEAD_PANELS[first:], first):
                    load_panel(8 * h + p - 1, p % 2, w_in[0], group * D + h * P)

            def load_small(dst, src):
                sp.dma_start(dst, src).then_inc(small_in, 16)

            for i in range(NT // 2):
                load_x(i)
            with nc.allow_non_contiguous_dma(reason="gains and biases, one value to a partition"):
                sp.dma_start(ng[:, :], norm_g[0].rearrange("(k p) -> p k", p=P)).then_inc(ng_in, 16)
            for p in range(2):
                load_panel(0, p, w_in[0], HEAD_PANELS[p] * D)
            for i in range(NT // 2, NT):
                load_x(i)
            with nc.allow_non_contiguous_dma(reason="gains and biases, one value to a partition"):
                load_small(lb_in[:, 0, :], lb_logits[0].rearrange("h p -> p h"))
                load_small(lb_in[:, 1, :], lb_logits[1].rearrange("h p -> p h"))
                load_small(hgn[:, :], hg_norm_g[0].rearrange("h p -> p h"))
                load_small(bg[:, :], b_gate[0].rearrange("(k p) -> p k", p=P))
            load_head(0, 2)
            load_head(1)
            with sp.Fori(0, 3) as i:
                load_head(2 * i + 2)
                load_head(2 * i + 3)
            for p in range(N_GATE_PANELS):
                load_panel(N_HEAD_PANELS + p - 1, p % 2, w_in[0], GATES * D + p * P)
            for first, source in ((SB_PANEL0, w_sb[0]), (HG_PANEL0, w_hg[0])):
                with sp.Fori(0, D // P // 2) as i:
                    for c in range(2):
                        load_panel(2 * i + (first + c - 1), c, source, (2 * i + c) * P)
            for e, column in enumerate(OUT_COLUMNS):
                load_panel(OUT_PANEL0 + e - 1, e % 2, w_out[0], column * P)
                if e == 3:
                    sp.wait_ge(proj_done, TAIL_SLOT0 + 4 * KT)
                    for i in range(NT):
                        sp.dma_start(x_again[:, i, :], x[0, i * P:(i + 1) * P, :]).then_inc(x_again_in, 16)
                    sp.wait_ge(gated, 4 * KT)
                    sp.dma_start(fg[:, :], final_g.rearrange("(a n) -> a n", a=1).broadcast_to([P, D])).then_inc(fg_in, 16)
            for i in range(NT):
                sp.wait_ge(normed, i + 1)
                sp.dma_start(out[0, i * P:(i + 1) * P, :], res[:, i, :]).then_inc(stored, 16)
            sp.wait_ge(stored, 16 * NT)

        @block.gpsimd
        def _(pool):
            nc.gpsimd.memset(ident[:, :], 0.0).then_inc(const_made, 1)
            pool.wait_ge(const_made, 1)
            nc.gpsimd.affine_select(out=ident[:, :], in_=ident[:, :], compare_op=ALU.not_equal, fill=1.0,
                                    base=0, pattern=[[-1, P]], channel_multiplier=1).then_inc(const_made, 1)
            nc.gpsimd.memset(mean_w[:, :].bitcast(F32), 1.0 / P).then_inc(const_made, 1)
            nc.gpsimd.memset(kappa[:, S:S + 1], 1.0).then_inc(const_made, 1)
            nc.gpsimd.memset(level_mask[:, :, :], 1.0).then_inc(const_made, 1)
            nc.gpsimd.memset(before[:, :], 1.0).then_inc(const_made, 1)
            nc.gpsimd.memset(not_before[:, :], 0.0).then_inc(const_made, 1)
            pool.wait_ge(const_made, 7)
            nc.gpsimd.affine_select(out=before[:, :], in_=before[:, :], compare_op=ALU.is_gt, fill=0.0,
                                    base=0, pattern=[[-1, P]], channel_multiplier=1).then_inc(const_made, 1)
            nc.gpsimd.affine_select(out=not_before[:, :], in_=not_before[:, :], compare_op=ALU.is_gt, fill=1.0,
                                    base=0, pattern=[[-1, P]], channel_multiplier=1).then_inc(const_made, 1)
            made = 9
            for level in range(MASKED):
                size = 1 << level
                pairs = P // 2 // size
                view = level_mask[:, level, :].rearrange("p (i b) -> p i b", b=size)
                nc.gpsimd.affine_select(out=view, in_=view, compare_op=ALU.is_ge, fill=0.0, base=0,
                                        pattern=[[-2 * size, pairs], [0, size]], channel_multiplier=1).then_inc(const_made, 1)
                made += 1
                pool.wait_ge(const_made, made)
                nc.gpsimd.affine_select(out=view, in_=view, compare_op=ALU.is_gt, fill=0.0, base=size,
                                        pattern=[[2 * size, pairs], [0, size]], channel_multiplier=-1).then_inc(const_made, 1)
                made += 1
            pool.wait_ge(const_made, made)

            def split(n, parity, slot):
                pool.wait_ge(w_hi_ready, n + 1)
                nc.gpsimd.tensor_tensor(w_lo[:, slot, :, :], w_raw[:, parity, :, :],
                                        w_hi[:, slot, :, :].bitcast(F32), ALU.subtract).then_inc(w_ready, 1)

            def split_out(e):
                pool.wait_ge(w_hi_ready, OUT_PANEL0 + e + 1)
                hi, lo = out_weights(OUT_COLUMNS[e])
                nc.gpsimd.tensor_tensor(lo, w_raw[:, e % 2, :, :], hi.bitcast(F32), ALU.subtract).then_inc(w_ready, 1)

            def step(h, splits):
                for u in range(SLOTS):
                    if u in splits:
                        p = splits[u]
                        slot = PANEL_SLOT[p] if splits is not GATE_SPLITS and p < 8 else p % 2
                        split(8 * h + p, p % 2, slot)

            split(0, 0, 0)
            split(1, 1, 1)
            step(0, {u: p for u, p in HEAD_SPLITS.items() if p > 1})
            step(1, HEAD_SPLITS)
            with pool.Fori(0, 3) as i:
                step(2 * i + 2, HEAD_SPLITS)
                step(2 * i + 3, HEAD_SPLITS)
            step(GATE_STEP, GATE_SPLITS)
            step(GATE_STEP + 1, GATE_SPLITS)
            with pool.Fori(0, 2 * KT // 2) as i:
                split(2 * i + (SB_PANEL0 + 1), 1, 1)
                split(2 * i + (SB_PANEL0 + 2), 0, 0)
            for e in range(1, KT):
                split_out(e)


        @block.scalar
        def _(act):
            act.wait_ge(const_made, IDENT_MADE)
            nc.scalar.activation(square_dump[:, 0:P], ident[:, :], ACT.Sqrt).then_inc(ss_done, 1)

            def split(parity, slot, loads_before):
                act.wait_ge(w_loaded[parity], 16 * loads_before + 16)
                nc.scalar.activation(w_hi[:, slot, :, :], w_raw[:, parity, :, :], ACT.Copy).then_inc(w_hi_ready, 1)

            def norm_tiles(first, n):
                for i in range(first, first + n):
                    act.wait_ge(x_in[i], 16)
                    act.wait_ge(ss_done, i + 1)
                    nc.scalar.activation(square_dump[:, :], x_tok[:, i, :], ACT.Square,
                                         accum_out=rstd[:, i:i + 1]).then_inc(ss_done, 1)
                    act.wait_ge(ss_done, i + 2)
                    nc.scalar.activation(rstd[:, i:i + 1], rstd[:, i:i + 1], ACT.Sqrt, scale=1.0 / D, bias=EPS).then_inc(rms_x, 1)

            def take_hT(half):
                for k in range(KT):
                    g = KT * half + k
                    act.wait_ge(xT_done, g + 1)
                    if g == 0:
                        act.wait_ge(ng_in, 16)
                    nc.scalar.activation(halfs(hT_hi[:, k, :], half), xT_bank(g), ACT.Copy,
                                         scale=ng[:, k:k + 1]).then_inc(hT_hi_ready, 1)

            norm_tiles(0, 4)
            split(0, 0, 0)
            take_hT(0)
            split(1, 1, 0)
            norm_tiles(4, 2)
            def evacuate(h, u, s, position):
                p, b = u // 2, u % 2
                act.wait_ge(proj_done, 16 * h + position + 1)
                if u == 0:
                    need(act, sb_split, 2 * (h - 1))
                group = HEAD_PANELS[p]
                if group in (SB_Q, SB_K):
                    nc.scalar.activation(halfs((qT if group == SB_Q else kT)[s], b), pj[b], ACT.Copy).then_inc(proj_free[b], 1)
                elif group == HG_F:
                    nc.scalar.activation(halfs(forget[s], b), pj[b], ACT.Sigmoid).then_inc(proj_free[b], 1)
                elif group in (SB_V, HG_I):
                    t = 2 * (u - 12)
                    nc.scalar.activation(vv[s][:, t:t + 2, :, :], pj[b].rearrange("p (t g e) -> p t g e", t=2, g=2),
                                         ACT.Copy).then_inc(proj_free[b], 1)
                else:
                    dst = {HG_Q: hq, SB_Z: zT, HG_Z: hzT}[group][s]
                    nc.scalar.activation(halfs(dst, b), pj[b], ACT.Sigmoid).then_inc(proj_sig, 1)

            def make_gate(r, u):
                p, b = u // 2, u % 2
                act.wait_ge(proj_done, 16 * (GATE_STEP + r) + u + 1)
                if r == 0 and u == 0:
                    act.wait_ge(sb_split, 2 * (HEADS - 1))
                need(act, gate_stored[b], 16 * (8 * r + p))
                nc.scalar.activation(gate_out[r][:, b, :], pj[b], ACT.Sigmoid,
                                     bias=bg[:, 8 * r + p:8 * r + p + 1]).then_inc(proj_free[b], 1)
                act.wait_ge(proj_free[b], 8 * (GATE_STEP + r) + p + 1)
                act.dma_start(halfs(gate_d[8 * r + p], b), gate_out[r][:, b, :]).then_inc(gate_stored[b], 16)

            def take_turned(a, j, part):
                g = tr_group(j, part)
                first = 4 * part
                n = min(4, j + 1 - first)
                act.wait_ge(wtr_done, 12 * a + g + 1)
                need(act, pv_done, 8 * a + j - 1)
                nc.scalar.activation(wT[:, j % 2, first:first + n, :], turned[:, 0:n * P], ACT.Copy).then_inc(wT_ready, 1)

            def sigmoids(a, j):
                n = (j + 1) * P
                act.wait_ge(qk_done, 8 * a + j + 1)
                nc.scalar.activation(beta[:, S - n:S], score[:, 0:n], ACT.Sigmoid, scale=SB_SCALE)
                nc.scalar.activation(kappa[:, S - n:S], score[:, 0:n], ACT.Sigmoid, scale=-SB_SCALE).then_inc(sig_done, 1)

            def attend_hg(a, u, s):
                if u == 8:
                    act.wait_ge(ktr_done, a + 1)
                    for b in range(2):
                        nc.scalar.activation(halfs(forget[s], b), halfs(hb, b), ACT.Copy).then_inc(kt_ready, 1)
                if u == 11:
                    act.wait_ge(ho_done, a + 1)
                    for b in range(2):
                        nc.scalar.activation(halfs(scT, b), halfs(hb, b), ACT.Square).then_inc(sq_done, 1)
                if u == 12:
                    act.wait_ge(hn_done, a + 1)
                    for b in range(2):
                        nc.scalar.activation(halfs(scT, b), halfs(hb, b), ACT.Sqrt, bias=EPS).then_inc(rms_done, 1)

            def store(what, a, b):
                split_sem, stored_sem, parts, dram = {"sb": (sb_split, sb_stored, sb_parts, osb_d),
                                                      "hg": (hg_split, hg_stored, hg_parts, ohg_d)}[what]
                act.wait_ge(split_sem, 2 * a + b + 1)
                act.dma_start(dram[a][:, :, b * HALF:(b + 1) * HALF], parts[:, :, :].bitcast(F32)).then_inc(stored_sem, 16)

            def step(h, attend, s, stores_before=True):
                gates = isinstance(h, int) and h >= GATE_STEP
                splits = GATE_SPLITS if gates else HEAD_SPLITS
                for u in range(SLOTS):
                    if attend and u in TR_SLOT and TR_SLOT[u] >= 4:
                        take_turned(h - 1, TR_SLOT[u], 0)
                    if gates:
                        make_gate(h - GATE_STEP, u)
                    else:
                        evacuate(h, u, s, u)
                    if attend and u in TR_SLOT:
                        take_turned(h - 1, TR_SLOT[u], 1 if TR_SLOT[u] >= 4 else 0)
                    if u in splits:
                        p = splits[u]
                        split(p % 2, PANEL_SLOT[p] if p < 8 and not gates else p % 2, 4 * h + p // 2)
                    if attend and u in QK_SLOT:
                        sigmoids(h - 1, QK_SLOT[u])
                    if u == 0 and stores_before:
                        store("sb", h - 2, 1)
                    if attend:
                        attend_hg(h - 1, u, 1 - s)
                        if u == 7:
                            store("sb", h - 1, 0)
                        if u >= 14:
                            store("hg", h - 1, u - 14)
                    if gates and not attend:
                        come_back(u)

            def come_back(u):
                if u == 2:
                    store("sb", HEADS - 1, 1)
                if u == 5:
                    act.wait_ge(sb_stored, 32 * HEADS)
                    act.wait_ge(hg_split, 2 * HEADS)
                if 5 <= u < 5 + HEADS:
                    for part, dst in enumerate((osb_hi, osb_lo)):
                        act.dma_start(dst[:, u - 5, :].bitcast(F32), osb_d[u - 5][:, part, :]).then_inc(osb_in, 16)
                if u == 13:
                    act.wait_ge(hg_stored, 32 * HEADS)
                    for b in range(2):
                        act.dma_start(gate_in[:, b, :], halfs(gate_d[0], b)).then_inc(gate_loaded[b], 16)

            for position, u in enumerate(START_ORDER):
                evacuate(0, u, 0, position)
                if position == 0:
                    norm_tiles(6, 2)
                if position == 1:
                    take_hT(1)
                    act.wait_ge(lb_step, 1)
                    nc.scalar.activation(lb[:, :], lb_in[:, 0, :], ACT.Sigmoid).then_inc(lb_step, 1)
                if position in HEAD_SPLITS and position > 0:
                    p = HEAD_SPLITS[position]
                    split(p % 2, PANEL_SLOT[p] if p < 8 else p % 2, p // 2)
            step(1, True, 1, False)
            with act.Fori(0, 3) as i:
                step(2 * i + 2, True, 0)
                step(2 * i + 3, True, 1)
            step(GATE_STEP, True, 0)
            step(GATE_STEP + 1, False, 1, False)
            for b in range(2):
                act.wait_ge(gate_stored[b], 16 * N_GATE_PANELS)

            def tail_panel(i, c, more):
                act.wait_ge(proj_done, 4 * i + (2 * c + TAIL_SLOT0))
                split(1 - c, 1 - c, i + (SB_PANEL0 // 2 + c))
                for b in range(2 if more else 0):
                    act.wait_ge(gated, 4 * i + (2 * c + b + 1))
                    act.dma_start(gate_in[:, b, :], gate_d[2 * i + (c + 1)][:, b * HALF:(b + 1) * HALF]).then_inc(gate_loaded[b], 16)

            def fetch_ohg(e):
                for part, dst in enumerate((ohg_hi, ohg_lo)):
                    act.dma_start(dst[:, bass.ds(e, 1), :].rearrange("p a n -> p (a n)").bitcast(F32),
                                  ohg_d[e][:, part, :]).then_inc(ohg_in, 16)

            with act.Fori(0, KT // 2) as i:
                for c in range(2):
                    fetch_ohg(2 * i + c)
                    tail_panel(i, c, True)
            with act.Fori(KT // 2, KT - 1) as i:
                tail_panel(i, 0, True)
                tail_panel(i, 1, True)
            tail_panel(KT - 1, 0, True)
            tail_panel(KT - 1, 1, False)
            for e in range(1, KT):
                if e == 3:
                    act.wait_ge(proj_done, TAIL_SLOT0 + 4 * KT)
                act.wait_ge(w_loaded[e % 2], 16 * ((OUT_PANEL0 + e) // 2) + 16)
                nc.scalar.activation(out_weights(OUT_COLUMNS[e])[0], w_raw[:, e % 2, :, :], ACT.Copy).then_inc(w_hi_ready, 1)
            for i in range(NT):
                act.wait_ge(res_ready, NT + i + 1)
                need(act, res_ss, i)
                nc.scalar.activation(last_dump[:, :], res[:, i, :], ACT.Square, accum_out=rstd[:, i:i + 1]).then_inc(res_ss, 1)
                act.wait_ge(res_ss, i + 1)
                nc.scalar.activation(rstd[:, i:i + 1], rstd[:, i:i + 1], ACT.Sqrt, scale=1.0 / D, bias=EPS).then_inc(res_rms, 1)

        @block.vector
        def _(dve):
            v = nc.vector
            for half in range(2):
                if half == 1:
                    dve.wait_ge(small_in, 16 * 4)
                    v.tensor_tensor(lb_in[:, 0, :], lb_in[:, 0, :], lb_in[:, 1, :], ALU.subtract).then_inc(lb_step, 1)
                for i in range(4 * half, 4 * half + 4):
                    dve.wait_ge(rms_x, i + 1)
                    v.reciprocal(rstd[:, i:i + 1], rstd[:, i:i + 1]).then_inc(rstd_ready, 1)
                    dve.wait_ge(rstd_ready, i + 1)
                    v.tensor_scalar(x_tok[:, i, :], x_tok[:, i, :], rstd[:, i:i + 1], None, ALU.mult).then_inc(xn_ready, 1)
                for k in range(KT):
                    g = KT * half + k
                    dve.wait_ge(hT_hi_ready, g + 1)
                    v.scalar_tensor_tensor(out=halfs(hT_lo[:, k, :], half), in0=xT_bank(g), scalar=ng[:, k:k + 1],
                                           in1=halfs(hT_hi[:, k, :], half).bitcast(F32), op0=ALU.mult, op1=ALU.subtract).then_inc(hT_ready, 1)
            dve.wait_ge(lb_step, 2)
            v.tensor_scalar(one_m_lb[:, :], lb[:, :], -1.0, 1.0, ALU.mult, ALU.add).then_inc(lb_step, 1)
            dve.wait_ge(lb_step, 3)

            def evacuate(h, u, s):
                p, b = u // 2, u % 2
                group = HEAD_PANELS[p]
                if group in (HG_Q, SB_Z, HG_Z):
                    dve.wait_ge(proj_sig, 6 * h + {HG_Q: 0, SB_Z: 2, HG_Z: 4}[group] + b + 1)
                    dst = halfs({HG_Q: hq, SB_Z: zT, HG_Z: hzT}[group][s], b)
                    v.tensor_tensor(dst, pj[b], dst, ALU.mult).then_inc(proj_free[b], 1)
                elif group == HG_F:
                    dve.wait_ge(proj_free[b], 8 * h + p + 1)
                    f = halfs(forget[s], b)
                    v.tensor_scalar(f, f, one_m_lb[:, bass.ds(h, 1)], lb[:, bass.ds(h, 1)], ALU.mult, ALU.add).then_inc(forget_ready, 1)
                    dve.wait_ge(forget_ready, 2 * h + b + 1)
                    v.tensor_scalar(halfs(hk[s], b), f, -1.0, 1.0, ALU.mult, ALU.add).then_inc(hk_ready, 1)

            def weigh(a, j):
                n = (j + 1) * P
                dve.wait_ge(sig_done, 8 * a + j + 1)
                v.tensor_tensor(kappa[:, S - P:S], kappa[:, S - P:S], not_before[:, :], ALU.max).then_inc(masked, 1)
                v.tensor_tensor(beta[:, S - P:S], beta[:, S - P:S], before[:, :], ALU.mult).then_inc(masked, 1)
                dve.wait_ge(masked, 16 * a + 2 * j + 2)
                back = kappa[:, S - n:S][:, ::-1]
                v.tensor_tensor_scan(back, back, back, 1.0, ALU.mult, ALU.min).then_inc(scan_done, 1)
                dve.wait_ge(scan_done, 8 * a + j + 1)
                v.tensor_tensor(beta[:, S - n:S], beta[:, S - n:S], kappa[:, S - n + 1:S + 1], ALU.mult).then_inc(w_done, 1)

            def finish_sb(a, b, s):
                dve.wait_ge(pv_done, 8 * a + 4 * b + 4)
                o = halfs(qT[s], b)
                v.tensor_tensor(o, attended, halfs(zT[s], b), ALU.mult).then_inc(sb_taken, 1)
                dve.wait_ge(sb_taken, 2 * a + b + 1)
                need(dve, sb_stored, 32 * a + 16 * b)
                v.tensor_copy(sb_parts[:, 0, :], o).then_inc(sb_hi, 1)
                dve.wait_ge(sb_hi, 2 * a + b + 1)
                v.tensor_tensor(sb_parts[:, 1, :], o, sb_parts[:, 0, :].bitcast(F32), ALU.subtract).then_inc(sb_split, 1)

            def finish_hg(a, b, s):
                o = halfs(hq[s], b)
                need(dve, hg_stored, 32 * a + 16 * b)
                v.tensor_copy(hg_parts[:, 0, :], o).then_inc(hg_hi, 1)
                dve.wait_ge(hg_hi, 2 * a + b + 1)
                v.tensor_tensor(hg_parts[:, 1, :], o, hg_parts[:, 0, :].bitcast(F32), ALU.subtract).then_inc(hg_split, 1)

            def grow(a, m, s):
                size = 1 << (m - 1)
                pairs = S // (2 * size)

                def pairs_of(t):
                    return t[s][:, :].rearrange("p (c two b) -> p c two b", two=2, b=size)

                even, odd = (pairs_of(forget)[:, :, z, 0:1] for z in range(2))
                q_odd, k_even = pairs_of(hq)[:, :, 1, :], pairs_of(hk)[:, :, 0, :]
                v.tensor_tensor(q_odd, q_odd, even.broadcast_to([P, pairs, size]), ALU.mult).then_inc(grown, 1)
                v.tensor_tensor(k_even, k_even, odd.broadcast_to([P, pairs, size]), ALU.mult).then_inc(grown, 1)
                return even, odd

            def multiply_totals(a, m, even, odd):
                dve.wait_ge(grown, 14 * a + 2 * m)
                total = chunk_total[:, :].unsqueeze(2) if m == LEVELS else even
                v.tensor_tensor(total, even, odd, ALU.mult).then_inc(decayed, 1)

            def attend_hg(a, u, s):
                if u == 0:
                    dve.wait_ge(hs_done, 8 * a + 1)
                    v.tensor_tensor(scT[:, :].rearrange("p (n t) -> p n t", n=NT), hb.rearrange("p (n t) -> p n t", n=NT),
                                    ident[:, :].unsqueeze(1).broadcast_to([P, NT, P]), ALU.mult).then_inc(hs_taken, 1)
                    v.tensor_tensor(hq[s][:, :], hq[s][:, :], forget[s][:, :], ALU.mult).then_inc(decayed, 1)
                if 1 <= u <= LEVELS:
                    size = 1 << (u - 1)
                    dve.wait_ge(hs_done, 8 * a + u + 1)
                    dve.wait_ge(decayed, 8 * a + u)
                    even, odd = grow(a, u, s)
                    half = halfs(hb, (u + 1) % 2)
                    chunks = scT[:, :].rearrange("p (n t) -> p n t", n=NT)
                    if size >= 32:
                        for first in range(0, P, 2 * size):
                            last = v.tensor_copy(chunks[first:first + size, :, first + size:first + 2 * size],
                                                 half.rearrange("p (n t) -> p n t", n=NT)[first:first + size, :, first // 2:first // 2 + size])
                        last.then_inc(hs_taken, 1)
                    else:
                        dve.wait_ge(const_made, CONSTANTS)
                        dve.wait_ge(hs_taken, 8 * a + u)
                        v.copy_predicated(chunks[0:P - size].rearrange("p n (i two b) -> p n i two b", two=2, b=size)[:, :, :, 1, :],
                                          level_mask[0:P - size, u - 1, :].bitcast(I32).rearrange("p (i b) -> p i b", b=size)
                                          .unsqueeze(1).broadcast_to([P - size, NT, P // 2 // size, size]),
                                          half[0:P - size].rearrange("p (n i b) -> p n i b", n=NT, b=size)).then_inc(hs_taken, 1)
                    multiply_totals(a, u, even, odd)
                if u == 9:
                    dve.wait_ge(kv_done, a + 1)
                    dve.wait_ge(decayed, 8 * a + 8)
                    for n in range(NT - 1):
                        new, kv = hk[s][:, n * P:(n + 1) * P], hb[:, n * P:(n + 1) * P]
                        if n == 0:
                            v.tensor_copy(new, kv).then_inc(state_step, 1)
                        else:
                            dve.wait_ge(state_step, 7 * a + n)
                            v.scalar_tensor_tensor(out=new, in0=hk[s][:, (n - 1) * P:n * P], scalar=chunk_total[:, n:n + 1],
                                                   in1=kv, op0=ALU.mult, op1=ALU.add).then_inc(state_step, 1)
                if u == 11:
                    for b in range(2):
                        dve.wait_ge(sq_done, 2 * a + b + 1)
                        v.tensor_scalar(halfs(hq[s], b), halfs(hb, b), hgn[:, bass.ds(a, 1)], None, ALU.mult).then_inc(on_done, 1)
                        v.tensor_copy(halfs(sq_hi[s], b), halfs(scT, b)).then_inc(sq_hi_ready, 1)
                        dve.wait_ge(sq_hi_ready, 2 * a + b + 1)
                        v.tensor_tensor(halfs(sq_lo[s], b), halfs(scT, b), halfs(sq_hi[s], b).bitcast(F32), ALU.subtract).then_inc(sq_split, 1)
                if u == 12:
                    dve.wait_ge(rms_done, 2 * a + 2)
                    v.reciprocal(scT[:, :], scT[:, :]).then_inc(hg_norm, 1)
                    dve.wait_ge(hg_norm, 3 * a + 1)
                    dve.wait_ge(on_done, 2 * a + 2)
                    v.tensor_tensor(hq[s][:, :], hq[s][:, :], scT[:, :], ALU.mult).then_inc(hg_norm, 1)
                    dve.wait_ge(hg_norm, 3 * a + 2)
                    v.tensor_tensor(hq[s][:, :], hq[s][:, :], hzT[s][:, :], ALU.mult).then_inc(hg_norm, 1)
                    dve.wait_ge(hg_norm, 3 * a + 3)
                if u in (13, 14):
                    finish_hg(a, u - 13, s)

            def step(h, attend, s):
                for u in range(SLOTS):
                    if not (isinstance(h, int) and h >= GATE_STEP):
                        evacuate(h, u, s)
                    if attend:
                        if u in QK_SLOT:
                            weigh(h - 1, QK_SLOT[u])
                        attend_hg(h - 1, u, 1 - s)
                        if u == 6:
                            finish_sb(h - 1, 0, 1 - s)
                        if u == 15:
                            finish_sb(h - 1, 1, 1 - s)

            for u in START_ORDER:
                evacuate(0, u, 0)
            dve.wait_ge(const_made, CONSTANTS)
            step(1, True, 1)
            with dve.Fori(0, 3) as i:
                step(2 * i + 2, True, 0)
                step(2 * i + 3, True, 1)
            step(GATE_STEP, True, 0)

            for b in range(2):
                dve.wait_ge(gate_stored[b], 16 * N_GATE_PANELS)

            def gate_sb(t, b, load):
                dve.wait_ge(proj_done, 2 * t + (TAIL_SLOT0 + b + 1))
                dve.wait_ge(gate_loaded[b], 16 * t + 16)
                dst = y_sum[:, t, b * HALF:(b + 1) * HALF] if isinstance(t, int) else y_sum[:, bass.ds(t, 1), b * HALF:(b + 1) * HALF].rearrange("p a n -> p (a n)")
                v.tensor_tensor(dst, pj[b], gate_in[:, b, :], ALU.mult).then_inc(gated, 1)

            with dve.Fori(0, KT) as t:
                gate_sb(t, 0, None)
                gate_sb(t, 1, None)
            with dve.Fori(0, KT) as t:
                for b in range(2):
                    dve.wait_ge(proj_done, 2 * t + (TAIL_SLOT0 + 2 * KT + b + 1))
                    dve.wait_ge(gate_loaded[b], 16 * t + (16 * KT + 16))
                    v.tensor_tensor(gate_in[:, b, :], pj[b], gate_in[:, b, :], ALU.mult).then_inc(y_part, 1)
                    dve.wait_ge(y_part, 2 * t + (b + 1))

                    def part(y):
                        return y[:, bass.ds(t, 1), b * HALF:(b + 1) * HALF].rearrange("p a n -> p (a n)")

                    v.tensor_tensor(part(y_sum), part(y_sum), gate_in[:, b, :], ALU.add).then_inc(gated, 1)
                    dve.wait_ge(gated, 2 * t + (2 * KT + b + 1))
                    v.tensor_copy(part(y_hi), part(y_sum)).then_inc(y_hi_ready, 1)
                    dve.wait_ge(y_hi_ready, 2 * t + (b + 1))
                    v.tensor_tensor(part(y_lo), part(y_sum), part(y_hi).bitcast(F32), ALU.subtract).then_inc(y_ready, 1)

            dve.wait_ge(x_again_in, 16 * NT)
            dve.wait_ge(y_ready, 2 * KT)

            def last_norm(i):
                dve.wait_ge(res_rms, i + 1)
                v.reciprocal(rstd[:, i:i + 1], rstd[:, i:i + 1]).then_inc(res_rstd, 1)
                dve.wait_ge(res_rstd, i + 1)
                v.scalar_tensor_tensor(out=res[:, i, :], in0=res[:, i, :], scalar=rstd[:, i:i + 1], in1=fg[:, :],
                                       op0=ALU.mult, op1=ALU.mult).then_inc(normed, 1)

            dve.wait_ge(fg_in, 16)
            for g in range(2 * NT):
                c, i = g // NT, g % NT
                dve.wait_ge(out_done, g + 1)
                cols = slice(c * HALF, (c + 1) * HALF)
                v.tensor_tensor(res[:, i, cols], out_bank(g), x_again[:, i, cols], ALU.add).then_inc(res_ready, 1)
                if g > NT:
                    last_norm(i - 1)
            last_norm(NT - 1)

        @block.tensor
        def _(pe):
            mm = nc.tensor.matmul
            pe.wait_ge(const_made, IDENT_MADE)
            def turn_x(tile, k):
                return nc.tensor.transpose(xT_bank(KT * (tile // 4) + k)[:, tile % 4 * P:(tile % 4 + 1) * P],
                                           x_tok[:, tile, k * P:(k + 1) * P], ident[:, :])

            for i in range(4):
                pe.wait_ge(xn_ready, i + 1)
                for k in range(KT):
                    last = turn_x(i, k)
                    if i == 3:
                        last.then_inc(xT_done, 1)

            def feature_major(b, slot, hi, lo, ready_from=None):
                for k in range(KT):
                    if ready_from is not None:
                        pe.wait_ge(hT_ready, ready_from + k + 1)
                    for z, (w, t) in enumerate(((w_hi, hi), (w_hi, lo), (w_lo, hi))):
                        last = mm(pj[b], w[:, slot, k, :], halfs(t[:, k, :], b), start=k == 0 and z == 0, stop=k == KT - 1 and z == 2)
                return last

            def token_major(b, t):
                for i in range(2):
                    dst = pj[b][:, i * 2 * P:(i + 1) * 2 * P].rearrange("p (g e) -> p g e", g=2)
                    for k in range(KT):
                        for z, (hh, w) in enumerate(((hT_hi, w_hi), (hT_lo, w_hi), (hT_hi, w_lo))):
                            last = mm(dst, hh[:, k, (t + i) * P:(t + i + 1) * P], w[:, 2:4, k, :],
                                      start=k == 0 and z == 0, stop=k == KT - 1 and z == 2)
                return last

            def project(h, u, gates, ready_from=None):
                p, b = u // 2, u % 2
                need(pe, proj_free[b], 8 * h + p)
                if u % 2 == 0:
                    pe.wait_ge(w_ready, 8 * h + p + (2 if u == 12 and not gates else 1))
                if u >= 12 and not gates:
                    last = token_major(b, 2 * (u - 12))
                else:
                    last = feature_major(b, p % 2, hT_hi, hT_lo, ready_from)
                last.then_inc(proj_done, 1)

            def scores(a, j, s):
                if j > 0:
                    pe.wait_ge(sig_done, 8 * a + j)
                n = (j + 1) * P
                for at in range(0, n, HALF):
                    m = min(HALF, n - at)
                    last = mm(score[:, at:at + m], qT[s][:, j * P:(j + 1) * P], kT[s][:, at:at + m], start=True, stop=True)
                last.then_inc(qk_done, 1)

            def turn(a, j, part):
                g = tr_group(j, part)
                pe.wait_ge(w_done, 8 * a + j + 1)
                need(pe, wT_ready, 12 * a + g)
                n = (j + 1) * P
                for i in range(4 * part, min(4 * part + 4, j + 1)):
                    last = nc.tensor.transpose(turned[:, (i % 4) * P:(i % 4 + 1) * P], beta[:, S - n + i * P:S - n + (i + 1) * P], ident[:, :])
                last.then_inc(wtr_done, 1)

            def attend_sb(a, j, s):
                pe.wait_ge(wT_ready, 12 * a + tr_group(j, 1 if j >= 4 else 0) + 1)
                if j % 4 == 0:
                    need(pe, sb_taken, 2 * a + j // 4)
                for i in range(j + 1):
                    last = mm(attended[:, (j % 4) * P:(j % 4 + 1) * P], vv[s][:, i, 0, :], wT[:, j % 2, i, :], start=i == 0, stop=i == j)
                last.then_inc(pv_done, 1)

            def attend_hg(a, u, s):
                def tile(t, n):
                    return t[:, n * P:(n + 1) * P]

                if u == 0:
                    pe.wait_ge(hk_ready, 2 * a + 2)
                    need(pe, rms_done, 2 * a)
                    for n in range(NT):
                        last = mm(tile(hb, n), tile(hk[s], n), tile(hq[s], n), start=True, stop=True)
                    last.then_inc(hs_done, 1)
                if 1 <= u <= LEVELS:
                    size = 1 << (u - 1)
                    pe.wait_ge(decayed, 8 * a + u)
                    pe.wait_ge(hs_taken, 8 * a + max(1, u - 1))
                    half = halfs(hb, (u + 1) % 2)
                    for n in range(NT):
                        if size >= 32:
                            for first in range(0, P, 2 * size):
                                keys = slice(n * P + first, n * P + first + size)
                                queries = slice(keys.stop, keys.stop + size)
                                column = n * 64 + first // 2
                                last = mm(half[first:first + size, column:column + size], hk[s][:, keys], hq[s][:, queries],
                                          start=True, stop=True)
                        else:
                            odd = tile(hq[s], n).rearrange("p (i two b) -> p i two b", two=2, b=size)[:, :, 1, :]
                            last = mm(half[0:P - size, n * 64:(n + 1) * 64].rearrange("p (i b) -> p i b", b=size),
                                      tile(hk[s], n)[:, 0:P - size], odd, start=True, stop=True)
                    last.then_inc(hs_done, 1)
                if u == 8:
                    pe.wait_ge(decayed, 8 * a + 8)
                    pe.wait_ge(hs_taken, 8 * a + 8)
                    for n in range(NT):
                        last = nc.tensor.transpose(tile(hb, n), tile(hk[s], n), ident[:, :])
                    last.then_inc(ktr_done, 1)
                if u == 9:
                    pe.wait_ge(kt_ready, 2 * a + 2)
                    for n in range(NT - 1):
                        last = mm(tile(hb, n), tile(forget[s], n), vv[s][:, n, 1, :], start=True, stop=True)
                    last.then_inc(kv_done, 1)
                if u == 11:
                    pe.wait_ge(state_step, 7 * a + 7)
                    for n in range(NT):
                        last = mm(tile(hb, n), vv[s][:, n, 1, :], tile(scT, n), start=True, stop=n == 0)
                        if n:
                            last = mm(tile(hb, n), tile(hk[s], n - 1), tile(hq[s], n), start=False, stop=True)
                    last.then_inc(ho_done, 1)
                if u == 12:
                    pe.wait_ge(sq_split, 2 * a + 2)
                    for b in range(2):
                        mm(halfs(hb, b), mean_w[:, :], halfs(sq_hi[s], b), start=True, stop=False)
                        last = mm(halfs(hb, b), mean_w[:, :], halfs(sq_lo[s], b), start=False, stop=True)
                    last.then_inc(hn_done, 1)

            def step(h, attend, s):
                gates = isinstance(h, int) and h >= GATE_STEP
                a, o = h - 1, 1 - s
                for u in range(SLOTS):
                    if attend and u in TR_SLOT and TR_SLOT[u] >= 4:
                        turn(a, TR_SLOT[u], 0)
                    project(h, u, gates)
                    if attend:
                        if u in TR_SLOT:
                            turn(a, TR_SLOT[u], 1 if TR_SLOT[u] >= 4 else 0)
                        if u in QK_SLOT:
                            scores(a, QK_SLOT[u], o)
                        if u in PV_SLOT:
                            attend_sb(a, PV_SLOT[u], o)
                        attend_hg(a, u, o)

            for u in START_ORDER:
                if u == 1:
                    for k in range(KT):
                        pe.wait_ge(xn_ready, NT)
                        pe.wait_ge(hT_ready, KT if k < 6 else KT + k - 5)
                        for i in range(4, NT):
                            last = turn_x(i, k)
                        last.then_inc(xT_done, 1)
                project(0, u, False, u * KT if u < 2 else None)
            pe.wait_ge(const_made, CONSTANTS)
            step(1, True, 1)
            with pe.Fori(0, 3) as i:
                step(2 * i + 2, True, 0)
                step(2 * i + 3, True, 1)
            step(GATE_STEP, True, 0)
            step(GATE_STEP + 1, False, 1)

            def branch_panel(t, c, first, hi, lo):
                pe.wait_ge(w_ready, t + (SB_PANEL0 + first + 1))
                for b in range(2):
                    if not (isinstance(t, int) and t + first == 0):
                        pe.wait_ge(gated, 2 * t + (2 * first + b - 1))
                    else:
                        pe.wait_ge(proj_free[b], TAIL_SLOT0 // 2)
                    feature_major(b, c, hi, lo).then_inc(proj_done, 1)

            pe.wait_ge(osb_in, 16 * 2 * HEADS)
            branch_panel(0, 0, 0, osb_hi, osb_lo)
            branch_panel(1, 1, 0, osb_hi, osb_lo)
            with pe.Fori(0, KT // 2 - 1) as i:
                branch_panel(2 * i + 2, 0, 0, osb_hi, osb_lo)
                branch_panel(2 * i + 3, 1, 0, osb_hi, osb_lo)
            pe.wait_ge(ohg_in, 16 * 2 * HEADS)
            with pe.Fori(0, KT // 2) as i:
                branch_panel(2 * i, 0, KT, ohg_hi, ohg_lo)
                branch_panel(2 * i + 1, 1, KT, ohg_hi, ohg_lo)

            for g in range(2 * NT):
                c, i = g // NT, g % NT
                if i == 0:
                    pe.wait_ge(w_ready, OUT_PANEL0 + 4 * (c + 1))
                need(pe, res_ready, g - 7)
                if g == 0:
                    pe.wait_ge(y_ready, 2 * KT - 2)
                dst = out_bank(g).rearrange("p (g e) -> p g e", g=4)
                for k in range(KT):
                    if k == KT - 1 and g in (0, NT // 2):
                        pe.wait_ge(y_ready, 2 * KT - 1 + g // (NT // 2))
                    hi, lo = (w_hi, w_lo) if c == 0 else (wo_hi, wo_lo)
                    for z, (y, w) in enumerate(((y_hi, hi), (y_lo, hi), (y_hi, lo))):
                        last = mm(dst, y[:, k, i * P:(i + 1) * P], w[:, :, k, :], start=k == 0 and z == 0, stop=k == KT - 1 and z == 2)
                last.then_inc(out_done, 1)


_INS = ("x", "norm_g", "w_in", "b_gate", "lb_logits", "hg_norm_g", "w_sb_proj", "w_hg_proj", "w_out", "final_norm_g")


def kernel(**inputs):
    import numpy as np
    import concourse.bacc as bacc
    from concourse.bass_utils import run_bass_kernel_spmd

    nc = bacc.Bacc("TRN2", target_bir_lowering=False, num_devices=1)
    arrays = {f"in_{name}": np.ascontiguousarray(inputs[name]) for name in _INS}
    args = [nc.dram_tensor(name, a.shape, mybir.dt.from_np(a.dtype), kind="ExternalInput").ap() for name, a in arrays.items()]
    out = nc.dram_tensor("out", (1, S, D), F32, kind="ExternalOutput").ap()
    build(nc, *args, out)
    r = run_bass_kernel_spmd(nc, [arrays], core_ids=[0])
    return r.results[0]["out"]
```

```python
from contextlib import ExitStack

import concourse.bass as bass
from concourse import mybir

F32 = mybir.dt.float32
F32R = mybir.dt.float32r
BF16 = mybir.dt.bfloat16
I32 = mybir.dt.int32
ACT = mybir.ActivationFunctionType
ALU = mybir.AluOpType

P = 128
D = 1024
S = 1024
KT = D // P
NT = S // P
HEADS = 8
HALF = S // 2
SLOTS = 16
EPS = 1e-6
SB_SCALE = float(P) ** -0.5
LEVELS = 7
MASKED = 5
IDENT_MADE = 2
CONSTANTS = 9 + 2 * MASKED
SBUF_BASE = 16512

SB_Q, SB_K, SB_V, SB_Z, HG_Q, HG_F, HG_I, HG_Z, GATES = range(9)
HEAD_PANELS = (SB_Q, SB_K, HG_Q, HG_F, SB_Z, HG_Z, SB_V, HG_I)
PANEL_SLOT = (0, 1, 0, 1, 0, 1, 2, 3)
GATE_STEP = HEADS
N_GATE_PANELS = 2 * D // P
N_HEAD_PANELS = HEADS * len(HEAD_PANELS)
SB_PANEL0 = N_HEAD_PANELS + N_GATE_PANELS
HG_PANEL0 = SB_PANEL0 + D // P
OUT_PANEL0 = HG_PANEL0 + D // P
TAIL_SLOT0 = 10 * SLOTS

HEAD_SPLITS = {0: 1, 2: 2, 4: 3, 6: 4, 8: 5, 9: 6, 10: 7, 12: 8}
GATE_SPLITS = {0: 1, 2: 2, 4: 3, 6: 4, 8: 5, 10: 6, 12: 7, 14: 8}

START_ORDER = (0, 2, 1, 3) + tuple(range(4, SLOTS))

OUT_COLUMNS = (2, 3, 0, 1, 4, 5, 6, 7)
LAST_HG_PANEL = HG_PANEL0 + D // P - 1 + 2


def out_panel(e):
    return OUT_PANEL0 + e - (1 if e < 2 else 0)


NORM_PIECES = [(i, slice(0, D)) for i in range(NT - 1)] + [(NT - 1, slice(0, HALF)), (NT - 1, slice(HALF, D))]

QK_SLOT = {0: 0, 1: 1, 2: 2, 3: 3, 5: 4, 7: 5, 9: 6, 11: 7}
TR_SLOT = {1: 0, 2: 1, 3: 2, 4: 3, 7: 4, 9: 5, 11: 6, 13: 7}
PV_SLOT = {2: 0, 3: 1, 4: 2, 5: 3, 8: 4, 10: 5, 12: 6, 14: 7}


def tr_group(j, part):
    return j if j < 4 else 4 + 2 * (j - 4) + part


def need(engine, semaphore, value):
    if isinstance(value, int) and value <= 0:
        return
    engine.wait_ge(semaphore, value)


def build(nc, x, norm_g, w_in, b_gate, lb_logits, hg_norm_g, w_sb, w_hg, w_out, final_g, out):
    ctx = ExitStack()
    with ctx:
        def sem(name):
            return ctx.enter_context(nc.semaphore(name))

        def place(name, offset, free, dt=F32):
            return nc.alloc_sbuf_tensor_at(name, [P] + list(free), dt, offset=SBUF_BASE + offset)

        KB = 1024
        hT_hi = place("hT_hi", 0, [KT, S], F32R)
        hT_lo = place("hT_lo", 32 * KB, [KT, S], F32R)
        ohg_hi = place("ohg_hi", 0, [KT, S], F32R)
        ohg_lo = place("ohg_lo", 32 * KB, [KT, S], F32R)
        ohg_raw = place("ohg_raw", 32 * KB, [KT, S])
        wo_hi = place("wo_hi", 0, [4, KT, P], F32R)
        wo_lo = place("wo_lo", 16 * KB, [4, KT, P], F32R)
        x_again = place("x_again", 32 * KB, [NT, D])
        w_raw = place("w_raw", 64 * KB, [2, KT, P])
        w_hi = place("w_hi", 72 * KB, [4, KT, P], F32R)
        w_lo = place("w_lo", 88 * KB, [4, KT, P], F32R)
        WORK = 104 * KB
        SET = 36 * KB

        def in_sets(name, at, free, dt=F32):
            return [place(f"{name}{i}", WORK + i * SET + at * KB, free, dt) for i in range(2)]

        qT = in_sets("qT", 0, [S])
        q_lo = in_sets("q_lo", 0, [S], F32R)
        k_hi = in_sets("k_hi", 4, [S], F32R)
        vv = in_sets("vv", 8, [NT, 2, P])
        zT = in_sets("zT", 16, [S])
        hzT = in_sets("hzT", 20, [S])
        hq = in_sets("hq", 24, [S])
        hk = in_sets("hk", 28, [S])
        forget = in_sets("forget", 32, [S])
        sq_lo = in_sets("sq_lo", 28, [S], F32R)
        sq_hi = in_sets("sq_hi", 32, [S], F32R)
        at = WORK + 2 * SET
        beta = place("beta", at, [S])
        kappa = place("kappa", at + 4096, [S + 1])
        wT = place("wT", at + 8224, [2, NT, P])
        scT = place("scT", at + 16416, [S])
        qk_hi = place("qk_hi", at + 8224 + 4096, [S], F32R)
        qk_lo = place("qk_lo", at + 16416, [S], F32R)
        k_lo = [place(f"k_lo{i}", at + 20512 + 4096 * i, [S], F32R) for i in range(2)]
        q_hi = place("q_hi", at + 28704, [P], F32R)
        at += 28704 + 512
        ident = place("ident", at, [P])
        mean_w = place("mean_w", at + 512, [P], F32R)
        level_mask = place("level_mask", at + 1024, [MASKED, P // 2])
        at += 1024 + MASKED * 256
        ng = place("ng", at, [KT])
        lb = place("lb", at + 32, [HEADS])
        one_m_lb = place("one_m_lb", at + 64, [HEADS])
        hgn = place("hgn", at + 96, [HEADS])
        bg = place("bg", at + 128, [N_GATE_PANELS])
        chunk_total = place("chunk_total", at + 192, [NT])
        rstd = place("rstd", at + 224, [NT])
        left_ss = place("left_ss", at + 192, [NT])
        lb_in = place("lb_in", at + 256, [2, HEADS])
        before = place("before", at + 320, [P], BF16)
        not_before = place("not_before", at + 576, [P], BF16)
        x_tok = place("x_tok", WORK, [NT, D])
        square_dump = place("square_dump", WORK + 32 * KB, [D])
        osb_hi = place("osb_hi", WORK, [KT, S], F32R)
        osb_lo = place("osb_lo", WORK + 32 * KB, [KT, S], F32R)
        osb_raw = place("osb_raw", WORK + 32 * KB, [KT, S])
        y_hi = place("y_hi", WORK, [KT, S], F32R)
        y_lo = place("y_lo", WORK + 32 * KB, [KT, S], F32R)
        y_sum = place("y_sum", WORK + 64 * KB, [KT, S])
        res = place("res", WORK + 64 * KB, [NT, D])
        gate_in = place("gate_in", WORK + 96 * KB, [2, HALF])
        fg = place("fg", WORK + 96 * KB, [D])
        last_dump = place("last_dump", 64 * KB, [HALF])
        gate_out = [place("gate_out0", WORK, [2, HALF]), place("gate_out1", WORK + 64 * KB, [2, HALF])]

        osb_d = nc.dram_tensor("osb_d", (HEADS, P, S), F32, kind="Internal").ap()
        ohg_d = nc.dram_tensor("ohg_d", (HEADS, P, S), F32, kind="Internal").ap()
        gate_d = nc.dram_tensor("gate_d", (N_GATE_PANELS, P, S), F32, kind="Internal").ap()

        banks = ctx.enter_context(nc.psum_tensor("banks", [P, 8, HALF], F32))
        pj = [banks[:, 0, :], banks[:, 1, :]]
        score = banks[:, 2:4, :].rearrange("p a n -> p (a n)")
        turned = banks[:, 4, :]
        attended = banks[:, 5, :]
        hb = banks[:, 6:8, :].rearrange("p a n -> p (a n)")

        x_in = [sem(f"x_in{i}") for i in range(NT)]
        small_in = sem("small_in")
        ng_in = sem("ng_in")
        const_made = sem("const_made")
        ss_done = sem("ss_done")
        rms_x = sem("rms_x")
        rstd_ready = sem("rstd_ready")
        xn_ready = sem("xn_ready")
        xT_done = sem("xT_done")
        hT_hi_ready = sem("hT_hi_ready")
        hT_ready = sem("hT_ready")
        lb_step = sem("lb_step")
        w_loaded = [sem("w_loaded0"), sem("w_loaded1")]
        w_hi_ready = sem("w_hi_ready")
        w_ready = sem("w_ready")
        proj_done = sem("proj_done")
        proj_sig = sem("proj_sig")
        proj_free = [sem("proj_free0"), sem("proj_free1")]
        forget_ready = sem("forget_ready")
        hk_ready = sem("hk_ready")
        qk_done = sem("qk_done")
        sig_done = sem("sig_done")
        masked = sem("masked")
        scan_done = sem("scan_done")
        w_done = sem("w_done")
        wtr_done = sem("wtr_done")
        wT_ready = sem("wT_ready")
        pv_done = sem("pv_done")
        sb_taken = sem("sb_taken")
        k_hi_ready = sem("k_hi_ready")
        q_hi_ready = sem("q_hi_ready")
        q_split = sem("q_split")
        o_hi_ready = sem("o_hi_ready")
        osb_split = sem("osb_split")
        ohg_split = sem("ohg_split")
        sb_stored = sem("sb_stored")
        qk_step = sem("qk_step")
        hs_done = sem("hs_done")
        hs_taken = sem("hs_taken")
        grown = sem("grown")
        decayed = sem("decayed")
        ktr_done = sem("ktr_done")
        kt_ready = sem("kt_ready")
        kv_done = sem("kv_done")
        state_step = sem("state_step")
        ho_done = sem("ho_done")
        sq_done = sem("sq_done")
        sq_hi_ready = sem("sq_hi_ready")
        sq_split = sem("sq_split")
        on_done = sem("on_done")
        hn_done = sem("hn_done")
        rms_done = sem("rms_done")
        hg_norm = sem("hg_norm")
        hg_stored = sem("hg_stored")
        gate_made = sem("gate_made")
        gate_stored = [sem("gate_stored0"), sem("gate_stored1")]
        osb_in = sem("osb_in")
        ohg_in = [sem("ohg_in0"), sem("ohg_in1")]
        gate_loaded = [sem("gate_loaded0"), sem("gate_loaded1")]
        gated = sem("gated")
        y_part = sem("y_part")
        y_hi_ready = sem("y_hi_ready")
        y_ready = sem("y_ready")
        x_again_in = sem("x_again_in")
        fg_in = sem("fg_in")
        out_done = sem("out_done")
        res_ready = sem("res_ready")
        res_ss = sem("res_ss")
        left_done = sem("left_done")
        left_mean = sem("left_mean")
        res_rms = sem("res_rms")
        res_rstd = sem("res_rstd")
        normed = sem("normed")
        stored = sem("stored")

        block = ctx.enter_context(nc.Block())

        def halfs(t, b):
            return t[:, b * HALF:(b + 1) * HALF]

        def out_weights(column):
            if column < 4:
                return w_hi[:, column, :, :], w_lo[:, column, :, :]
            return wo_hi[:, column - 4, :, :], wo_lo[:, column - 4, :, :]

        def xT_bank(g):
            return banks[:, g if g < KT else 2 + (g - KT) % 6, :]

        def out_bank(g):
            return banks[:, (g + 2) % 8, :]

        def by_rows(w):
            return w.rearrange("(k p) e -> p k e", p=P)

        @block.sync
        def _(sp):
            def load_x(i):
                sp.dma_start(x_tok[:, i, :], x[0, i * P:(i + 1) * P, :]).then_inc(x_in[i], 16)

            def load_panel(n_before, parity, source, first):
                need(sp, w_ready, n_before)
                sp.dma_start(w_raw[:, parity, :, :], by_rows(source)[:, :, bass.ds(first, P)]).then_inc(w_loaded[parity], 16)

            def load_head(h, first=0):
                for p, group in enumerate(HEAD_PANELS[first:], first):
                    load_panel(8 * h + p - 1, p % 2, w_in[0], group * D + h * P)

            def load_small(dst, src):
                sp.dma_start(dst, src).then_inc(small_in, 16)

            for i in range(NT // 2):
                load_x(i)
            with nc.allow_non_contiguous_dma(reason="gains and biases, one value to a partition"):
                sp.dma_start(ng[:, :], norm_g[0].rearrange("(k p) -> p k", p=P)).then_inc(ng_in, 16)
            for p in range(2):
                load_panel(0, p, w_in[0], HEAD_PANELS[p] * D)
            for i in range(NT // 2, NT):
                load_x(i)
            with nc.allow_non_contiguous_dma(reason="gains and biases, one value to a partition"):
                load_small(lb_in[:, 0, :], lb_logits[0].rearrange("h p -> p h"))
                load_small(lb_in[:, 1, :], lb_logits[1].rearrange("h p -> p h"))
                load_small(hgn[:, :], hg_norm_g[0].rearrange("h p -> p h"))
                load_small(bg[:, :], b_gate[0].rearrange("(k p) -> p k", p=P))
            load_head(0, 2)
            load_head(1)
            with sp.Fori(0, 3) as i:
                load_head(2 * i + 2)
                load_head(2 * i + 3)
            for p in range(N_GATE_PANELS):
                load_panel(N_HEAD_PANELS + p - 1, p % 2, w_in[0], GATES * D + p * P)
            for first, source, pairs in ((SB_PANEL0, w_sb[0], KT // 2), (HG_PANEL0, w_hg[0], KT // 2 - 1)):
                with sp.Fori(0, pairs) as i:
                    for c in range(2):
                        load_panel(2 * i + (first + c - 1), c, source, (2 * i + c) * P)
            load_panel(HG_PANEL0 + KT - 3, 0, w_hg[0], (KT - 2) * P)
            for e, column in enumerate(OUT_COLUMNS):
                if e == 2:
                    load_panel(LAST_HG_PANEL - 1, LAST_HG_PANEL % 2, w_hg[0], (KT - 1) * P)
                load_panel(out_panel(e) - 1, out_panel(e) % 2, w_out[0], column * P)
                if e == 3:
                    sp.wait_ge(proj_done, TAIL_SLOT0 + 4 * KT)
                    for i in range(NT):
                        sp.dma_start(x_again[:, i, :], x[0, i * P:(i + 1) * P, :]).then_inc(x_again_in, 16)
                    sp.wait_ge(gated, 4 * KT)
                    sp.dma_start(fg[:, :], final_g.rearrange("(a n) -> a n", a=1).broadcast_to([P, D])).then_inc(fg_in, 16)
            for done, (i, cols) in enumerate(NORM_PIECES):
                sp.wait_ge(normed, done + 1)
                sp.dma_start(out[0, i * P:(i + 1) * P, cols], res[:, i, cols]).then_inc(stored, 16)
            sp.wait_ge(stored, 16 * len(NORM_PIECES))

        @block.gpsimd
        def _(pool):
            nc.gpsimd.memset(ident[:, :], 0.0).then_inc(const_made, 1)
            pool.wait_ge(const_made, 1)
            nc.gpsimd.affine_select(out=ident[:, :], in_=ident[:, :], compare_op=ALU.not_equal, fill=1.0,
                                    base=0, pattern=[[-1, P]], channel_multiplier=1).then_inc(const_made, 1)
            nc.gpsimd.memset(mean_w[:, :].bitcast(F32), 1.0 / P).then_inc(const_made, 1)
            nc.gpsimd.memset(kappa[:, S:S + 1], 1.0).then_inc(const_made, 1)
            nc.gpsimd.memset(level_mask[:, :, :], 1.0).then_inc(const_made, 1)
            nc.gpsimd.memset(before[:, :], 1.0).then_inc(const_made, 1)
            nc.gpsimd.memset(not_before[:, :], 0.0).then_inc(const_made, 1)
            pool.wait_ge(const_made, 7)
            nc.gpsimd.affine_select(out=before[:, :], in_=before[:, :], compare_op=ALU.is_gt, fill=0.0,
                                    base=0, pattern=[[-1, P]], channel_multiplier=1).then_inc(const_made, 1)
            nc.gpsimd.affine_select(out=not_before[:, :], in_=not_before[:, :], compare_op=ALU.is_gt, fill=1.0,
                                    base=0, pattern=[[-1, P]], channel_multiplier=1).then_inc(const_made, 1)
            made = 9
            for level in range(MASKED):
                size = 1 << level
                pairs = P // 2 // size
                view = level_mask[:, level, :].rearrange("p (i b) -> p i b", b=size)
                nc.gpsimd.affine_select(out=view, in_=view, compare_op=ALU.is_ge, fill=0.0, base=0,
                                        pattern=[[-2 * size, pairs], [0, size]], channel_multiplier=1).then_inc(const_made, 1)
                made += 1
                pool.wait_ge(const_made, made)
                nc.gpsimd.affine_select(out=view, in_=view, compare_op=ALU.is_gt, fill=0.0, base=size,
                                        pattern=[[2 * size, pairs], [0, size]], channel_multiplier=-1).then_inc(const_made, 1)
                made += 1
            pool.wait_ge(const_made, made)

            def split(n, parity, slot):
                pool.wait_ge(w_hi_ready, n + 1)
                nc.gpsimd.tensor_tensor(w_lo[:, slot, :, :], w_raw[:, parity, :, :],
                                        w_hi[:, slot, :, :].bitcast(F32), ALU.subtract).then_inc(w_ready, 1)

            def split_out(e):
                n = out_panel(e)
                pool.wait_ge(w_hi_ready, n + 1)
                hi, lo = out_weights(OUT_COLUMNS[e])
                nc.gpsimd.tensor_tensor(lo, w_raw[:, n % 2, :, :], hi.bitcast(F32), ALU.subtract).then_inc(w_ready, 1)

            def step(h, splits):
                for u in range(SLOTS):
                    if u in splits:
                        p = splits[u]
                        slot = PANEL_SLOT[p] if splits is not GATE_SPLITS and p < 8 else p % 2
                        split(8 * h + p, p % 2, slot)

            split(0, 0, 0)
            split(1, 1, 1)
            step(0, {u: p for u, p in HEAD_SPLITS.items() if p > 1})
            step(1, HEAD_SPLITS)
            with pool.Fori(0, 3) as i:
                step(2 * i + 2, HEAD_SPLITS)
                step(2 * i + 3, HEAD_SPLITS)
            step(GATE_STEP, GATE_SPLITS)
            step(GATE_STEP + 1, GATE_SPLITS)
            with pool.Fori(0, KT - 1) as i:
                split(2 * i + (SB_PANEL0 + 1), 1, 1)
                split(2 * i + (SB_PANEL0 + 2), 0, 0)
            for e in range(KT):
                if e == 2:
                    split(LAST_HG_PANEL, LAST_HG_PANEL % 2, 1)
                split_out(e)


        @block.scalar
        def _(act):
            act.wait_ge(const_made, IDENT_MADE)
            nc.scalar.activation(square_dump[:, 0:P], ident[:, :], ACT.Sqrt).then_inc(ss_done, 1)

            def split(parity, slot, loads_before):
                act.wait_ge(w_loaded[parity], 16 * loads_before + 16)
                nc.scalar.activation(w_hi[:, slot, :, :], w_raw[:, parity, :, :], ACT.Copy).then_inc(w_hi_ready, 1)

            def norm_tiles(first, n):
                for i in range(first, first + n):
                    act.wait_ge(x_in[i], 16)
                    act.wait_ge(ss_done, i + 1)
                    nc.scalar.activation(square_dump[:, :], x_tok[:, i, :], ACT.Square,
                                         accum_out=rstd[:, i:i + 1]).then_inc(ss_done, 1)
                    act.wait_ge(ss_done, i + 2)
                    nc.scalar.activation(rstd[:, i:i + 1], rstd[:, i:i + 1], ACT.Sqrt, scale=1.0 / D, bias=EPS).then_inc(rms_x, 1)

            def take_hT(half):
                for k in range(KT):
                    g = KT * half + k
                    act.wait_ge(xT_done, g + 1)
                    if g == 0:
                        act.wait_ge(ng_in, 16)
                    nc.scalar.activation(halfs(hT_hi[:, k, :], half), xT_bank(g), ACT.Copy,
                                         scale=ng[:, k:k + 1]).then_inc(hT_hi_ready, 1)

            norm_tiles(0, 4)
            split(0, 0, 0)
            take_hT(0)
            split(1, 1, 0)
            norm_tiles(4, 2)
            def set_free(h, u):
                if u == 0:
                    need(act, sb_taken, 2 * (h - 1))
                    need(act, sb_stored, 16 * (2 * h - 3))
                if u == 1:
                    need(act, sb_stored, 16 * (2 * h - 2))
                if u == 4:
                    need(act, hg_stored, 16 * (2 * h - 2))

            def evacuate(h, u, s, position):
                p, b = u // 2, u % 2
                act.wait_ge(proj_done, 16 * h + position + 1)
                if u in (0, 1, 4):
                    set_free(h, u)
                group = HEAD_PANELS[p]
                if group == SB_Q:
                    nc.scalar.activation(halfs(qT[s], b), pj[b], ACT.Copy).then_inc(proj_free[b], 1)
                elif group == SB_K:
                    nc.scalar.activation(halfs(k_hi[s], b), pj[b], ACT.Copy).then_inc(k_hi_ready, 1)
                elif group == HG_F:
                    nc.scalar.activation(halfs(forget[s], b), pj[b], ACT.Sigmoid).then_inc(proj_free[b], 1)
                elif group in (SB_V, HG_I):
                    t = 2 * (u - 12)
                    nc.scalar.activation(vv[s][:, t:t + 2, :, :], pj[b].rearrange("p (t g e) -> p t g e", t=2, g=2),
                                         ACT.Copy).then_inc(proj_free[b], 1)
                else:
                    dst = {HG_Q: hq, SB_Z: zT, HG_Z: hzT}[group][s]
                    nc.scalar.activation(halfs(dst, b), pj[b], ACT.Sigmoid).then_inc(proj_sig, 1)

            def make_gate(r, u):
                p, b = u // 2, u % 2
                act.wait_ge(proj_done, 16 * (GATE_STEP + r) + u + 1)
                if r == 0 and u < 2:
                    set_free(HEADS, u)
                need(act, gate_stored[b], 16 * (8 * r + p))
                nc.scalar.activation(gate_out[r][:, b, :], pj[b], ACT.Sigmoid,
                                     bias=bg[:, 8 * r + p:8 * r + p + 1]).then_inc(proj_free[b], 1)
                act.wait_ge(proj_free[b], 8 * (GATE_STEP + r) + p + 1)
                act.dma_start(halfs(gate_d[8 * r + p], b), gate_out[r][:, b, :]).then_inc(gate_stored[b], 16)

            def take_turned(a, j, part):
                g = tr_group(j, part)
                first = 4 * part
                n = min(4, j + 1 - first)
                act.wait_ge(wtr_done, 12 * a + g + 1)
                need(act, pv_done, 8 * a + j - 1)
                nc.scalar.activation(wT[:, j % 2, first:first + n, :], turned[:, 0:n * P], ACT.Copy).then_inc(wT_ready, 1)

            def sigmoids(a, j):
                n = (j + 1) * P
                act.wait_ge(qk_done, 8 * a + j + 1)
                nc.scalar.activation(beta[:, S - n:S], score[:, 0:n], ACT.Sigmoid, scale=SB_SCALE)
                nc.scalar.activation(kappa[:, S - n:S], score[:, 0:n], ACT.Sigmoid, scale=-SB_SCALE).then_inc(sig_done, 1)

            def attend_hg(a, u, s):
                if u == 8:
                    act.wait_ge(ktr_done, a + 1)
                    for b in range(2):
                        nc.scalar.activation(halfs(forget[s], b), halfs(hb, b), ACT.Copy).then_inc(kt_ready, 1)
                if u == 11:
                    act.wait_ge(ho_done, a + 1)
                    for b in range(2):
                        nc.scalar.activation(halfs(scT, b), halfs(hb, b), ACT.Square).then_inc(sq_done, 1)
                if u == 12:
                    act.wait_ge(hn_done, a + 1)
                    for b in range(2):
                        nc.scalar.activation(halfs(scT, b), halfs(hb, b), ACT.Sqrt, bias=EPS).then_inc(rms_done, 1)

            def store_sb(a, b, s):
                act.wait_ge(sb_taken, 2 * a + b + 1)
                act.dma_start(halfs(osb_d[a], b), halfs(qT[s], b)).then_inc(sb_stored, 16)

            def store_hg(a, b, s):
                act.wait_ge(hg_norm, 3 * a + 3)
                act.dma_start(halfs(ohg_d[a], b), halfs(hq[s], b)).then_inc(hg_stored, 16)

            def step(h, attend, s, stores_before=True):
                gates = isinstance(h, int) and h >= GATE_STEP
                splits = GATE_SPLITS if gates else HEAD_SPLITS
                for u in range(SLOTS):
                    if attend and u in TR_SLOT and TR_SLOT[u] >= 4:
                        take_turned(h - 1, TR_SLOT[u], 0)
                    if gates:
                        make_gate(h - GATE_STEP, u)
                    else:
                        evacuate(h, u, s, u)
                    if attend and u in TR_SLOT:
                        take_turned(h - 1, TR_SLOT[u], 1 if TR_SLOT[u] >= 4 else 0)
                    if u in splits:
                        p = splits[u]
                        split(p % 2, PANEL_SLOT[p] if p < 8 and not gates else p % 2, 4 * h + p // 2)
                    if attend and u in QK_SLOT:
                        sigmoids(h - 1, QK_SLOT[u])
                    if u == 0 and stores_before:
                        store_sb(h - 2, 1, s)
                    if attend:
                        attend_hg(h - 1, u, 1 - s)
                        if u == 7:
                            store_sb(h - 1, 0, 1 - s)
                        if u >= 14:
                            store_hg(h - 1, u - 14, 1 - s)
                    if gates and not attend:
                        come_back(u)

            def come_back(u):
                if u == 2:
                    store_sb(HEADS - 1, 1, 1)
                if u == 4:
                    act.wait_ge(sb_stored, 32 * HEADS)
                    act.wait_ge(hg_stored, 32 * HEADS)
                if 4 <= u < 4 + HEADS // 2:
                    for e in (2 * u - 8, 2 * u - 7):
                        act.dma_start(osb_raw[:, e, :], osb_d[e]).then_inc(osb_in, 16)
                if u == 13:
                    for b in range(2):
                        act.dma_start(gate_in[:, b, :], halfs(gate_d[0], b)).then_inc(gate_loaded[b], 16)

            for position, u in enumerate(START_ORDER):
                evacuate(0, u, 0, position)
                if position == 0:
                    norm_tiles(6, 2)
                if position == 1:
                    take_hT(1)
                    act.wait_ge(lb_step, 1)
                    nc.scalar.activation(lb[:, :], lb_in[:, 0, :], ACT.Sigmoid).then_inc(lb_step, 1)
                if position in HEAD_SPLITS and position > 0:
                    p = HEAD_SPLITS[position]
                    split(p % 2, PANEL_SLOT[p] if p < 8 else p % 2, p // 2)
            step(1, True, 1, False)
            with act.Fori(0, 3) as i:
                step(2 * i + 2, True, 0)
                step(2 * i + 3, True, 1)
            step(GATE_STEP, True, 0)
            step(GATE_STEP + 1, False, 1, False)
            for b in range(2):
                act.wait_ge(gate_stored[b], 16 * N_GATE_PANELS)

            def split_out(e):
                n = out_panel(e)
                act.wait_ge(w_loaded[n % 2], 16 * (n // 2) + 16)
                nc.scalar.activation(out_weights(OUT_COLUMNS[e])[0], w_raw[:, n % 2, :, :], ACT.Copy).then_inc(w_hi_ready, 1)

            def fetch_gates(i, c):
                for b in range(2):
                    act.wait_ge(gated, 4 * i + (2 * c + b + 1))
                    act.dma_start(gate_in[:, b, :], gate_d[2 * i + (c + 1)][:, b * HALF:(b + 1) * HALF]).then_inc(gate_loaded[b], 16)

            def tail_panel(i, c):
                act.wait_ge(proj_done, 4 * i + (2 * c + TAIL_SLOT0))
                split(1 - c, 1 - c, i + (SB_PANEL0 // 2 + c))
                fetch_gates(i, c)

            def fetch_ohg(e, parity):
                act.dma_start(ohg_raw[:, bass.ds(e, 1), :].rearrange("p a n -> p (a n)"), ohg_d[e]).then_inc(ohg_in[parity], 16)

            with act.Fori(0, KT // 2) as i:
                for c in range(2):
                    fetch_ohg(2 * i + c, c)
                    tail_panel(i, c)
            with act.Fori(KT // 2, KT - 2) as i:
                tail_panel(i, 0)
                tail_panel(i, 1)
            tail_panel(KT - 2, 0)
            act.wait_ge(proj_done, TAIL_SLOT0 + 4 * (KT - 2) + 2)
            split(0, 0, (HG_PANEL0 + KT - 2) // 2)
            split_out(0)
            fetch_gates(KT - 2, 1)
            split_out(1)
            act.wait_ge(proj_done, TAIL_SLOT0 + 4 * (KT - 1))
            split(1, 1, LAST_HG_PANEL // 2)
            fetch_gates(KT - 1, 0)
            act.wait_ge(proj_done, TAIL_SLOT0 + 4 * (KT - 1) + 2)
            split_out(2)
            act.wait_ge(proj_done, TAIL_SLOT0 + 4 * KT)
            for e in range(3, KT):
                split_out(e)
            act.wait_ge(w_ready, OUT_PANEL0 + KT)
            for i in range(NT):
                act.wait_ge(res_ready, i + 1)
                need(act, left_done, i)
                nc.scalar.activation(last_dump[:, :], res[:, i, 0:HALF], ACT.Square, accum_out=left_ss[:, i:i + 1]).then_inc(left_done, 1)
            act.wait_ge(left_done, NT)
            act.wait_ge(left_mean, 1)
            for i in range(NT):
                act.wait_ge(res_ready, NT + i + 1)
                need(act, res_ss, i)
                nc.scalar.activation(last_dump[:, :], res[:, i, HALF:D], ACT.Square, accum_out=rstd[:, i:i + 1]).then_inc(res_ss, 1)
                act.wait_ge(res_ss, i + 1)
                nc.scalar.activation(rstd[:, i:i + 1], rstd[:, i:i + 1], ACT.Sqrt, scale=1.0 / D, bias=left_ss[:, i:i + 1]).then_inc(res_rms, 1)

        @block.vector
        def _(dve):
            v = nc.vector
            for half in range(2):
                if half == 1:
                    dve.wait_ge(small_in, 16 * 4)
                    v.tensor_tensor(lb_in[:, 0, :], lb_in[:, 0, :], lb_in[:, 1, :], ALU.subtract).then_inc(lb_step, 1)
                for i in range(4 * half, 4 * half + 4):
                    dve.wait_ge(rms_x, i + 1)
                    v.reciprocal(rstd[:, i:i + 1], rstd[:, i:i + 1]).then_inc(rstd_ready, 1)
                    dve.wait_ge(rstd_ready, i + 1)
                    v.tensor_scalar(x_tok[:, i, :], x_tok[:, i, :], rstd[:, i:i + 1], None, ALU.mult).then_inc(xn_ready, 1)
                for k in range(KT):
                    g = KT * half + k
                    dve.wait_ge(hT_hi_ready, g + 1)
                    v.scalar_tensor_tensor(out=halfs(hT_lo[:, k, :], half), in0=xT_bank(g), scalar=ng[:, k:k + 1],
                                           in1=halfs(hT_hi[:, k, :], half).bitcast(F32), op0=ALU.mult, op1=ALU.subtract).then_inc(hT_ready, 1)
            dve.wait_ge(lb_step, 2)
            v.tensor_scalar(one_m_lb[:, :], lb[:, :], -1.0, 1.0, ALU.mult, ALU.add).then_inc(lb_step, 1)
            dve.wait_ge(lb_step, 3)

            def evacuate(h, u, s):
                p, b = u // 2, u % 2
                group = HEAD_PANELS[p]
                if group == SB_K:
                    dve.wait_ge(k_hi_ready, 2 * h + b + 1)
                    v.tensor_tensor(halfs(k_lo[s], b), pj[b], halfs(k_hi[s], b).bitcast(F32), ALU.subtract).then_inc(proj_free[b], 1)
                if group in (HG_Q, SB_Z, HG_Z):
                    dve.wait_ge(proj_sig, 6 * h + {HG_Q: 0, SB_Z: 2, HG_Z: 4}[group] + b + 1)
                    dst = halfs({HG_Q: hq, SB_Z: zT, HG_Z: hzT}[group][s], b)
                    v.tensor_tensor(dst, pj[b], dst, ALU.mult).then_inc(proj_free[b], 1)
                elif group == HG_F:
                    dve.wait_ge(proj_free[b], 8 * h + p + 1)
                    f = halfs(forget[s], b)
                    v.tensor_scalar(f, f, one_m_lb[:, bass.ds(h, 1)], lb[:, bass.ds(h, 1)], ALU.mult, ALU.add).then_inc(forget_ready, 1)
                    dve.wait_ge(forget_ready, 2 * h + b + 1)
                    v.tensor_scalar(halfs(hk[s], b), f, -1.0, 1.0, ALU.mult, ALU.add).then_inc(hk_ready, 1)

            def split_q(a, j, s):
                tile = slice(j * P, (j + 1) * P)
                v.tensor_copy(q_hi[:, :], qT[s][:, tile]).then_inc(q_hi_ready, 1)
                dve.wait_ge(q_hi_ready, 8 * a + j + 1)
                v.tensor_tensor(q_lo[s][:, tile], qT[s][:, tile], q_hi[:, :].bitcast(F32), ALU.subtract).then_inc(q_split, 1)

            def weigh(a, j, s):
                n = (j + 1) * P
                dve.wait_ge(sig_done, 8 * a + j + 1)
                if j + 1 < NT:
                    split_q(a, j + 1, s)
                v.tensor_tensor(kappa[:, S - P:S], kappa[:, S - P:S], not_before[:, :], ALU.max).then_inc(masked, 1)
                v.tensor_tensor(beta[:, S - P:S], beta[:, S - P:S], before[:, :], ALU.mult).then_inc(masked, 1)
                dve.wait_ge(masked, 16 * a + 2 * j + 2)
                back = kappa[:, S - n:S][:, ::-1]
                v.tensor_tensor_scan(back, back, back, 1.0, ALU.mult, ALU.min).then_inc(scan_done, 1)
                dve.wait_ge(scan_done, 8 * a + j + 1)
                v.tensor_tensor(beta[:, S - n:S], beta[:, S - n:S], kappa[:, S - n + 1:S + 1], ALU.mult).then_inc(w_done, 1)

            def finish_sb(a, b, s):
                dve.wait_ge(pv_done, 8 * a + 4 * b + 4)
                v.tensor_tensor(halfs(qT[s], b), attended, halfs(zT[s], b), ALU.mult).then_inc(sb_taken, 1)

            def grow(a, m, s):
                size = 1 << (m - 1)
                pairs = S // (2 * size)

                def pairs_of(t):
                    return t[s][:, :].rearrange("p (c two b) -> p c two b", two=2, b=size)

                even, odd = (pairs_of(forget)[:, :, z, 0:1] for z in range(2))
                q_odd, k_even = pairs_of(hq)[:, :, 1, :], pairs_of(hk)[:, :, 0, :]
                v.tensor_tensor(q_odd, q_odd, even.broadcast_to([P, pairs, size]), ALU.mult).then_inc(grown, 1)
                v.tensor_tensor(k_even, k_even, odd.broadcast_to([P, pairs, size]), ALU.mult).then_inc(grown, 1)
                return even, odd

            def multiply_totals(a, m, even, odd):
                dve.wait_ge(grown, 14 * a + 2 * m)
                total = chunk_total[:, :].unsqueeze(2) if m == LEVELS else even
                v.tensor_tensor(total, even, odd, ALU.mult).then_inc(decayed, 1)

            def multiply_qk(a, s):
                dve.wait_ge(hk_ready, 2 * a + 2)
                v.tensor_tensor(scT[:, :], hq[s][:, :], hk[s][:, :], ALU.mult).then_inc(qk_step, 1)
                dve.wait_ge(qk_step, 3 * a + 1)
                v.tensor_copy(qk_hi[:, :], scT[:, :]).then_inc(qk_step, 1)
                dve.wait_ge(qk_step, 3 * a + 2)
                v.tensor_tensor(qk_lo[:, :], scT[:, :], qk_hi[:, :].bitcast(F32), ALU.subtract).then_inc(qk_step, 1)
                v.tensor_tensor(hq[s][:, :], hq[s][:, :], forget[s][:, :], ALU.mult).then_inc(decayed, 1)

            def attend_hg(a, u, s):
                if u == 0:
                    dve.wait_ge(hs_done, 8 * a + 1)
                    v.scalar_tensor_tensor(out=scT[:, :].rearrange("p (n t) -> p n t", n=NT), in0=hb.rearrange("p (n t) -> p n t", n=NT),
                                           scalar=float(P), in1=ident[:, :].unsqueeze(1).broadcast_to([P, NT, P]),
                                           op0=ALU.mult, op1=ALU.mult).then_inc(hs_taken, 1)
                if 1 <= u <= LEVELS:
                    size = 1 << (u - 1)
                    dve.wait_ge(hs_done, 8 * a + u + 1)
                    dve.wait_ge(decayed, 8 * a + u)
                    even, odd = grow(a, u, s)
                    half = halfs(hb, (u + 1) % 2)
                    chunks = scT[:, :].rearrange("p (n t) -> p n t", n=NT)
                    if size >= 32:
                        for first in range(0, P, 2 * size):
                            last = v.tensor_copy(chunks[first:first + size, :, first + size:first + 2 * size],
                                                 half.rearrange("p (n t) -> p n t", n=NT)[first:first + size, :, first // 2:first // 2 + size])
                        last.then_inc(hs_taken, 1)
                    else:
                        dve.wait_ge(const_made, CONSTANTS)
                        dve.wait_ge(hs_taken, 8 * a + u)
                        v.copy_predicated(chunks[0:P - size].rearrange("p n (i two b) -> p n i two b", two=2, b=size)[:, :, :, 1, :],
                                          level_mask[0:P - size, u - 1, :].bitcast(I32).rearrange("p (i b) -> p i b", b=size)
                                          .unsqueeze(1).broadcast_to([P - size, NT, P // 2 // size, size]),
                                          half[0:P - size].rearrange("p (n i b) -> p n i b", n=NT, b=size)).then_inc(hs_taken, 1)
                    multiply_totals(a, u, even, odd)
                if u == 9:
                    dve.wait_ge(kv_done, a + 1)
                    dve.wait_ge(decayed, 8 * a + 8)
                    for n in range(NT - 1):
                        new, kv = hk[s][:, n * P:(n + 1) * P], hb[:, n * P:(n + 1) * P]
                        if n == 0:
                            v.tensor_copy(new, kv).then_inc(state_step, 1)
                        else:
                            dve.wait_ge(state_step, 7 * a + n)
                            v.scalar_tensor_tensor(out=new, in0=hk[s][:, (n - 1) * P:n * P], scalar=chunk_total[:, n:n + 1],
                                                   in1=kv, op0=ALU.mult, op1=ALU.add).then_inc(state_step, 1)
                if u == 11:
                    for b in range(2):
                        dve.wait_ge(sq_done, 2 * a + b + 1)
                        v.tensor_scalar(halfs(hq[s], b), halfs(hb, b), hgn[:, bass.ds(a, 1)], None, ALU.mult).then_inc(on_done, 1)
                        v.tensor_copy(halfs(sq_hi[s], b), halfs(scT, b)).then_inc(sq_hi_ready, 1)
                        dve.wait_ge(sq_hi_ready, 2 * a + b + 1)
                        v.tensor_tensor(halfs(sq_lo[s], b), halfs(scT, b), halfs(sq_hi[s], b).bitcast(F32), ALU.subtract).then_inc(sq_split, 1)
                if u == 12:
                    dve.wait_ge(rms_done, 2 * a + 2)
                    v.reciprocal(scT[:, :], scT[:, :]).then_inc(hg_norm, 1)
                    dve.wait_ge(hg_norm, 3 * a + 1)
                    dve.wait_ge(on_done, 2 * a + 2)
                    v.tensor_tensor(hq[s][:, :], hq[s][:, :], scT[:, :], ALU.mult).then_inc(hg_norm, 1)
                    dve.wait_ge(hg_norm, 3 * a + 2)
                    v.tensor_tensor(hq[s][:, :], hq[s][:, :], hzT[s][:, :], ALU.mult).then_inc(hg_norm, 1)

            def step(h, attend, s):
                for b in range(2):
                    dve.wait_ge(proj_free[b], 8 * (h - 1) + 1)
                split_q(h - 1, 0, 1 - s)
                for u in range(SLOTS):
                    if not (isinstance(h, int) and h >= GATE_STEP):
                        evacuate(h, u, s)
                    if attend:
                        if u in QK_SLOT:
                            weigh(h - 1, QK_SLOT[u], 1 - s)
                        attend_hg(h - 1, u, 1 - s)
                        if u == 6:
                            finish_sb(h - 1, 0, 1 - s)
                        if u == 15:
                            finish_sb(h - 1, 1, 1 - s)
                if not (isinstance(h, int) and h >= GATE_STEP):
                    multiply_qk(h, s)

            for u in START_ORDER:
                evacuate(0, u, 0)
            multiply_qk(0, 0)
            dve.wait_ge(const_made, CONSTANTS)
            step(1, True, 1)
            with dve.Fori(0, 3) as i:
                step(2 * i + 2, True, 0)
                step(2 * i + 3, True, 1)
            step(GATE_STEP, True, 0)

            def split_branch(raw, hi, lo, done, e, hi_before):
                def tile(t):
                    return t[:, bass.ds(e, 1), :].rearrange("p a n -> p (a n)")

                v.tensor_copy(tile(hi), tile(raw)).then_inc(o_hi_ready, 1)
                dve.wait_ge(o_hi_ready, e + (hi_before + 1))
                v.tensor_tensor(tile(lo), tile(raw), tile(hi).bitcast(F32), ALU.subtract).then_inc(done, 1)

            for b in range(2):
                dve.wait_ge(gate_stored[b], 16 * N_GATE_PANELS // 2)
            dve.wait_ge(osb_in, 16 * KT)
            with dve.Fori(0, KT) as e:
                split_branch(osb_raw, osb_hi, osb_lo, osb_split, e, 0)

            for b in range(2):
                dve.wait_ge(gate_stored[b], 16 * N_GATE_PANELS)

            def gate_sb(t, b):
                dve.wait_ge(proj_done, 2 * t + (TAIL_SLOT0 + b + 1))
                dve.wait_ge(gate_loaded[b], 16 * t + 16)
                dst = y_sum[:, bass.ds(t, 1), b * HALF:(b + 1) * HALF].rearrange("p a n -> p (a n)")
                v.tensor_tensor(dst, pj[b], gate_in[:, b, :], ALU.mult).then_inc(gated, 1)

            with dve.Fori(0, KT // 2) as i:
                for c in range(2):
                    dve.wait_ge(ohg_in[c], 16 * i + 16)
                    split_branch(ohg_raw, ohg_hi, ohg_lo, ohg_split, 2 * i + c, KT)
                    gate_sb(2 * i + c, 0)
                    gate_sb(2 * i + c, 1)
            with dve.Fori(0, KT) as t:
                for b in range(2):
                    dve.wait_ge(proj_done, 2 * t + (TAIL_SLOT0 + 2 * KT + b + 1))
                    dve.wait_ge(gate_loaded[b], 16 * t + (16 * KT + 16))
                    v.tensor_tensor(gate_in[:, b, :], pj[b], gate_in[:, b, :], ALU.mult).then_inc(y_part, 1)
                    dve.wait_ge(y_part, 2 * t + (b + 1))

                    def part(y):
                        return y[:, bass.ds(t, 1), b * HALF:(b + 1) * HALF].rearrange("p a n -> p (a n)")

                    v.tensor_tensor(part(y_sum), part(y_sum), gate_in[:, b, :], ALU.add).then_inc(gated, 1)
                    dve.wait_ge(gated, 2 * t + (2 * KT + b + 1))
                    v.tensor_copy(part(y_hi), part(y_sum)).then_inc(y_hi_ready, 1)
                    dve.wait_ge(y_hi_ready, 2 * t + (b + 1))
                    v.tensor_tensor(part(y_lo), part(y_sum), part(y_hi).bitcast(F32), ALU.subtract).then_inc(y_ready, 1)

            dve.wait_ge(x_again_in, 16 * NT)
            dve.wait_ge(y_ready, 2 * KT)

            def last_norm(i):
                dve.wait_ge(res_rms, i + 1)
                v.reciprocal(rstd[:, i:i + 1], rstd[:, i:i + 1]).then_inc(res_rstd, 1)
                dve.wait_ge(res_rstd, i + 1)
                for cols in (cols for tile, cols in NORM_PIECES if tile == i):
                    v.scalar_tensor_tensor(out=res[:, i, cols], in0=res[:, i, cols], scalar=rstd[:, i:i + 1], in1=fg[:, cols],
                                           op0=ALU.mult, op1=ALU.mult).then_inc(normed, 1)

            dve.wait_ge(fg_in, 16)
            for g in range(2 * NT):
                c, i = g // NT, g % NT
                dve.wait_ge(out_done, g + 1)
                cols = slice(c * HALF, (c + 1) * HALF)
                v.tensor_tensor(res[:, i, cols], out_bank(g), x_again[:, i, cols], ALU.add).then_inc(res_ready, 1)
                if g == NT:
                    dve.wait_ge(left_done, NT)
                    v.tensor_scalar(left_ss[:, :], left_ss[:, :], 1.0 / D, EPS, ALU.mult, ALU.add).then_inc(left_mean, 1)
                if g >= NT:
                    last_norm(i)

        @block.tensor
        def _(pe):
            mm = nc.tensor.matmul
            pe.wait_ge(const_made, IDENT_MADE)
            def turn_x(tile, k):
                return nc.tensor.transpose(xT_bank(KT * (tile // 4) + k)[:, tile % 4 * P:(tile % 4 + 1) * P],
                                           x_tok[:, tile, k * P:(k + 1) * P], ident[:, :])

            for i in range(4):
                pe.wait_ge(xn_ready, i + 1)
                for k in range(KT):
                    last = turn_x(i, k)
                    if i == 3:
                        last.then_inc(xT_done, 1)

            def feature_major(b, slot, hi, lo, ready_from=None):
                for k in range(KT):
                    if ready_from is not None:
                        pe.wait_ge(hT_ready, ready_from + k + 1)
                    for z, (w, t) in enumerate(((w_hi, hi), (w_hi, lo), (w_lo, hi))):
                        last = mm(pj[b], w[:, slot, k, :], halfs(t[:, k, :], b), start=k == 0 and z == 0, stop=k == KT - 1 and z == 2)
                return last

            def token_major(b, t):
                for i in range(2):
                    dst = pj[b][:, i * 2 * P:(i + 1) * 2 * P].rearrange("p (g e) -> p g e", g=2)
                    for k in range(KT):
                        for z, (hh, w) in enumerate(((hT_hi, w_hi), (hT_lo, w_hi), (hT_hi, w_lo))):
                            last = mm(dst, hh[:, k, (t + i) * P:(t + i + 1) * P], w[:, 2:4, k, :],
                                      start=k == 0 and z == 0, stop=k == KT - 1 and z == 2)
                return last

            def project(h, u, gates, ready_from=None):
                p, b = u // 2, u % 2
                need(pe, proj_free[b], 8 * h + p)
                if u % 2 == 0:
                    pe.wait_ge(w_ready, 8 * h + p + (2 if u == 12 and not gates else 1))
                if u >= 12 and not gates:
                    last = token_major(b, 2 * (u - 12))
                else:
                    last = feature_major(b, p % 2, hT_hi, hT_lo, ready_from)
                last.then_inc(proj_done, 1)

            def scores(a, j, s):
                pe.wait_ge(q_split, 8 * a + j + 1)
                if j > 0:
                    pe.wait_ge(sig_done, 8 * a + j)
                n = (j + 1) * P
                low = q_lo[s][:, j * P:(j + 1) * P]
                for at in range(0, n, HALF):
                    m = min(HALF, n - at)
                    for z, (q, k) in enumerate(((q_hi[:, :], k_hi), (q_hi[:, :], k_lo), (low, k_hi))):
                        last = mm(score[:, at:at + m], q, k[s][:, at:at + m], start=z == 0, stop=z == 2)
                last.then_inc(qk_done, 1)

            def turn(a, j, part):
                g = tr_group(j, part)
                pe.wait_ge(w_done, 8 * a + j + 1)
                need(pe, wT_ready, 12 * a + g)
                n = (j + 1) * P
                for i in range(4 * part, min(4 * part + 4, j + 1)):
                    last = nc.tensor.transpose(turned[:, (i % 4) * P:(i % 4 + 1) * P], beta[:, S - n + i * P:S - n + (i + 1) * P], ident[:, :])
                last.then_inc(wtr_done, 1)

            def attend_sb(a, j, s):
                pe.wait_ge(wT_ready, 12 * a + tr_group(j, 1 if j >= 4 else 0) + 1)
                if j % 4 == 0:
                    need(pe, sb_taken, 2 * a + j // 4)
                for i in range(j + 1):
                    last = mm(attended[:, (j % 4) * P:(j % 4 + 1) * P], vv[s][:, i, 0, :], wT[:, j % 2, i, :], start=i == 0, stop=i == j)
                last.then_inc(pv_done, 1)

            def attend_hg(a, u, s):
                def tile(t, n):
                    return t[:, n * P:(n + 1) * P]

                if u == 0:
                    pe.wait_ge(qk_step, 3 * a + 3)
                    need(pe, rms_done, 2 * a)
                    for b in range(2):
                        mm(halfs(hb, b), mean_w[:, :], halfs(qk_hi, b), start=True, stop=False)
                        last = mm(halfs(hb, b), mean_w[:, :], halfs(qk_lo, b), start=False, stop=True)
                    last.then_inc(hs_done, 1)
                if 1 <= u <= LEVELS:
                    size = 1 << (u - 1)
                    pe.wait_ge(decayed, 8 * a + u)
                    pe.wait_ge(hs_taken, 8 * a + max(1, u - 1))
                    half = halfs(hb, (u + 1) % 2)
                    for n in range(NT):
                        if size >= 32:
                            for first in range(0, P, 2 * size):
                                keys = slice(n * P + first, n * P + first + size)
                                queries = slice(keys.stop, keys.stop + size)
                                column = n * 64 + first // 2
                                last = mm(half[first:first + size, column:column + size], hk[s][:, keys], hq[s][:, queries],
                                          start=True, stop=True)
                        else:
                            odd = tile(hq[s], n).rearrange("p (i two b) -> p i two b", two=2, b=size)[:, :, 1, :]
                            last = mm(half[0:P - size, n * 64:(n + 1) * 64].rearrange("p (i b) -> p i b", b=size),
                                      tile(hk[s], n)[:, 0:P - size], odd, start=True, stop=True)
                    last.then_inc(hs_done, 1)
                if u == 8:
                    pe.wait_ge(decayed, 8 * a + 8)
                    pe.wait_ge(hs_taken, 8 * a + 8)
                    for n in range(NT):
                        last = nc.tensor.transpose(tile(hb, n), tile(hk[s], n), ident[:, :])
                    last.then_inc(ktr_done, 1)
                if u == 9:
                    pe.wait_ge(kt_ready, 2 * a + 2)
                    for n in range(NT - 1):
                        last = mm(tile(hb, n), tile(forget[s], n), vv[s][:, n, 1, :], start=True, stop=True)
                    last.then_inc(kv_done, 1)
                if u == 11:
                    pe.wait_ge(state_step, 7 * a + 7)
                    for n in range(NT):
                        last = mm(tile(hb, n), vv[s][:, n, 1, :], tile(scT, n), start=True, stop=n == 0)
                        if n:
                            last = mm(tile(hb, n), tile(hk[s], n - 1), tile(hq[s], n), start=False, stop=True)
                    last.then_inc(ho_done, 1)
                if u == 12:
                    pe.wait_ge(sq_split, 2 * a + 2)
                    for b in range(2):
                        mm(halfs(hb, b), mean_w[:, :], halfs(sq_hi[s], b), start=True, stop=False)
                        last = mm(halfs(hb, b), mean_w[:, :], halfs(sq_lo[s], b), start=False, stop=True)
                    last.then_inc(hn_done, 1)

            def step(h, attend, s):
                gates = isinstance(h, int) and h >= GATE_STEP
                a, o = h - 1, 1 - s
                for u in range(SLOTS):
                    if attend and u in TR_SLOT and TR_SLOT[u] >= 4:
                        turn(a, TR_SLOT[u], 0)
                    project(h, u, gates)
                    if attend:
                        if u in TR_SLOT:
                            turn(a, TR_SLOT[u], 1 if TR_SLOT[u] >= 4 else 0)
                        if u in QK_SLOT:
                            scores(a, QK_SLOT[u], o)
                        if u in PV_SLOT:
                            attend_sb(a, PV_SLOT[u], o)
                        attend_hg(a, u, o)

            for u in START_ORDER:
                if u == 1:
                    for k in range(KT):
                        pe.wait_ge(xn_ready, NT)
                        pe.wait_ge(hT_ready, KT if k < 6 else KT + k - 5)
                        for i in range(4, NT):
                            last = turn_x(i, k)
                        last.then_inc(xT_done, 1)
                project(0, u, False, u * KT if u < 2 else None)
            pe.wait_ge(const_made, CONSTANTS)
            step(1, True, 1)
            with pe.Fori(0, 3) as i:
                step(2 * i + 2, True, 0)
                step(2 * i + 3, True, 1)
            step(GATE_STEP, True, 0)
            step(GATE_STEP + 1, False, 1)

            def branch_panel(t, c, first, hi, lo, panel=None):
                pe.wait_ge(w_ready, t + (SB_PANEL0 + first + 1) if panel is None else panel + 1)
                for b in range(2):
                    if not (isinstance(t, int) and t + first == 0):
                        pe.wait_ge(gated, 2 * t + (2 * first + b - 1))
                    else:
                        pe.wait_ge(proj_free[b], TAIL_SLOT0 // 2)
                    feature_major(b, c, hi, lo).then_inc(proj_done, 1)

            pe.wait_ge(osb_split, KT)
            branch_panel(0, 0, 0, osb_hi, osb_lo)
            branch_panel(1, 1, 0, osb_hi, osb_lo)
            with pe.Fori(0, KT // 2 - 1) as i:
                branch_panel(2 * i + 2, 0, 0, osb_hi, osb_lo)
                branch_panel(2 * i + 3, 1, 0, osb_hi, osb_lo)
            pe.wait_ge(ohg_split, KT)
            with pe.Fori(0, KT // 2 - 1) as i:
                branch_panel(2 * i, 0, KT, ohg_hi, ohg_lo)
                branch_panel(2 * i + 1, 1, KT, ohg_hi, ohg_lo)
            branch_panel(KT - 2, 0, KT, ohg_hi, ohg_lo)
            branch_panel(KT - 1, 1, KT, ohg_hi, ohg_lo, LAST_HG_PANEL)

            def out_group(g, first, n):
                c, i = g // NT, g % NT
                hi, lo = (w_hi, w_lo) if c == 0 else (wo_hi, wo_lo)
                dst = out_bank(g)[:, first * P:(first + n) * P].rearrange("p (g e) -> p g e", g=n)
                for k in range(KT):
                    for z, (y, w) in enumerate(((y_hi, hi), (y_lo, hi), (y_hi, lo))):
                        last = mm(dst, y[:, k, i * P:(i + 1) * P], w[:, first:first + n, k, :], start=k == 0 and z == 0, stop=k == KT - 1 and z == 2)
                return last

            pe.wait_ge(y_ready, 2 * KT - 1)
            for g in range(2):
                out_group(g, 2, 2)
            pe.wait_ge(w_ready, OUT_PANEL0 + 4)
            for g in range(2):
                out_group(g, 0, 2).then_inc(out_done, 1)
            for g in range(2, 2 * NT):
                if g == NT // 2:
                    pe.wait_ge(y_ready, 2 * KT)
                if g == NT:
                    pe.wait_ge(w_ready, OUT_PANEL0 + KT)
                need(pe, res_ready, g - 7)
                out_group(g, 0, 4).then_inc(out_done, 1)


_INS = ("x", "norm_g", "w_in", "b_gate", "lb_logits", "hg_norm_g", "w_sb_proj", "w_hg_proj", "w_out", "final_norm_g")


def kernel(**inputs):
    import numpy as np
    import concourse.bacc as bacc
    from concourse.bass_utils import run_bass_kernel_spmd

    nc = bacc.Bacc("TRN2", target_bir_lowering=False, num_devices=1)
    arrays = {f"in_{name}": np.ascontiguousarray(inputs[name]) for name in _INS}
    args = [nc.dram_tensor(name, a.shape, mybir.dt.from_np(a.dtype), kind="ExternalInput").ap() for name, a in arrays.items()]
    out = nc.dram_tensor("out", (1, S, D), F32, kind="ExternalOutput").ap()
    build(nc, *args, out)
    r = run_bass_kernel_spmd(nc, [arrays], core_ids=[0])
    return r.results[0]["out"]
```
